# Optimizing a Trainium2 kernel written in Bass

```python
import jax, jax.numpy as jnp
from jax import lax
import numpy as np

D_MODEL = 1024
BATCH = 1
SEQ = 256
DEPTH = 1
DEC_BATCH = 8
DEC_SEQ = 1
PAST_LEN = 2048
PAGE_SIZE = 128

A_WIDTH = D_MODEL // 2
A_HEADS = 8
A_HEAD_DIM = A_WIDTH // A_HEADS
B_WIDTH = D_MODEL - A_WIDTH
B_GROUPS = 8
MIX_WIDTH = A_WIDTH + B_WIDTH
IN_WIDTH = 2 * A_WIDTH + 3 * B_WIDTH
CHUNK = 128
CONV_W = 3
N_MEM = 256
X_HEADS = 4
X_HEAD_DIM = D_MODEL // X_HEADS
N_EXPERTS = 32
TOP_K = 4
D_EXPERT = D_MODEL
SWIGLU_LIMIT = 7.0
SWIGLU_ALPHA = 1.702
MOE_BLOCK = 128
EPS = 1e-5

kernel_name = "hybrid_spatialgate_shortconv_memxattn_moe_step"

def rmsnorm(x, g):
    xf = x.astype(jnp.float32)
    r = lax.rsqrt(jnp.mean(xf * xf, axis=-1, keepdims=True) + EPS)
    return (xf * r).astype(x.dtype) * g

def spatial_gate(v, w_s, b_s):
    Bt, L, H, hd = v.shape
    Lp = -(-L // CHUNK) * CHUNK
    vp = jnp.pad(v, ((0, 0), (0, Lp - L), (0, 0), (0, 0)))
    vc = vp.reshape(Bt, Lp // CHUNK, CHUNK, H, hd)
    mask = jnp.tril(jnp.ones((CHUNK, CHUNK), dtype=bool))
    w = jnp.where(mask[None], w_s, jnp.zeros((), w_s.dtype))
    out = jnp.einsum('hts,bcshd->bcthd', w, vc) + b_s.T[None, None, :, :, None]
    return out.reshape(Bt, Lp, H, hd)[:, :L]

def mixer(h, conv_prev, w_in, g_v, w_s, b_s, w_conv, w_out):
    Bt, L, _ = h.shape
    proj = h @ w_in
    u, v, hb, bg, cg = jnp.split(
        proj, [A_WIDTH, 2 * A_WIDTH, 2 * A_WIDTH + B_WIDTH, 2 * A_WIDTH + 2 * B_WIDTH], axis=-1)
    u = jax.nn.gelu(u, approximate=False)
    v = jax.nn.gelu(v, approximate=False).reshape(Bt, L, A_HEADS, A_HEAD_DIM)
    v = rmsnorm(v, g_v)
    a_out = u * spatial_gate(v, w_s, b_s).reshape(Bt, L, A_WIDTH)
    z = cg * hb
    zcat = jnp.concatenate([conv_prev, z], axis=1)
    conv = zcat[:, 0:L] * w_conv[0]
    for k in range(1, CONV_W):
        conv = conv + zcat[:, k:k + L] * w_conv[k]
    b_out = bg * conv
    y = jnp.concatenate([a_out, b_out], axis=-1) @ w_out
    return y, v, zcat[:, L:]

def mem_kv(mem, g_mem, w_k, w_v):
    Bt = mem.shape[0]
    m = rmsnorm(mem, g_mem)
    k = (m @ w_k).reshape(Bt, N_MEM, X_HEADS, X_HEAD_DIM)
    v = (m @ w_v).reshape(Bt, N_MEM, X_HEADS, X_HEAD_DIM)
    return k, v

def cross_attn(h, k, v, w_q, w_xo):
    Bt, L, _ = h.shape
    q = (h @ w_q).reshape(Bt, L, X_HEADS, X_HEAD_DIM)
    s = jnp.einsum('bqhd,bkhd->bhqk', q, k).astype(jnp.float32) * (X_HEAD_DIM ** -0.5)
    p = jax.nn.softmax(s, axis=-1).astype(v.dtype)
    o = jnp.einsum('bhqk,bkhd->bqhd', p, v).reshape(Bt, L, D_MODEL)
    return o @ w_xo

def expert_ffn(xb, w1, b1, w2, b2):
    gu = xb @ w1 + b1
    gate, up = gu[:, :D_EXPERT], gu[:, D_EXPERT:]
    gate = jnp.minimum(gate, SWIGLU_LIMIT)
    up = jnp.clip(up, -SWIGLU_LIMIT, SWIGLU_LIMIT)
    glu = gate * jax.nn.sigmoid(gate * SWIGLU_ALPHA)
    return ((up + 1) * glu) @ w2 + b2

def moe(h, w_router, b_router, w1, b1, w2, b2):
    Bt, L, D = h.shape
    T = Bt * L
    xt = h.reshape(T, D)
    logits = (xt @ w_router).astype(jnp.float32) + b_router.astype(jnp.float32)
    top_logit, top_e = lax.top_k(logits, TOP_K)
    gates = jax.nn.softmax(top_logit, axis=-1)
    A = T * TOP_K
    flat_e = top_e.reshape(A).astype(jnp.int32)
    flat_tok = jnp.repeat(jnp.arange(T, dtype=jnp.int32), TOP_K)
    order = jnp.argsort(flat_e)
    sorted_e = flat_e[order]
    sorted_tok = flat_tok[order]
    sorted_gate = gates.reshape(A)[order]
    counts = jnp.bincount(flat_e, length=N_EXPERTS).astype(jnp.int32)
    starts = jnp.cumsum(counts) - counts
    padded = (counts + MOE_BLOCK - 1) // MOE_BLOCK * MOE_BLOCK
    pad_ends = jnp.cumsum(padded)
    pad_starts = pad_ends - padded
    dest = pad_starts[sorted_e] + (jnp.arange(A, dtype=jnp.int32) - starts[sorted_e])
    n_blocks = -(-A // MOE_BLOCK) + N_EXPERTS
    P = n_blocks * MOE_BLOCK
    row_tok = jnp.full((P,), T, dtype=jnp.int32).at[dest].set(sorted_tok)
    x_ext = jnp.concatenate([xt, jnp.zeros((1, D), xt.dtype)], axis=0)
    xb = x_ext[row_tok].reshape(n_blocks, MOE_BLOCK, D)
    block_e = jnp.minimum(
        jnp.searchsorted(pad_ends, jnp.arange(n_blocks, dtype=jnp.int32) * MOE_BLOCK, side='right'),
        N_EXPERTS - 1).astype(jnp.int32)

    def run_block(args):
        xblk, e = args
        return expert_ffn(xblk, w1[e], b1[e], w2[e], b2[e])

    yb = lax.map(run_block, (xb, block_e)).reshape(P, D)
    contrib = yb[dest] * sorted_gate[:, None].astype(yb.dtype)
    out = jax.ops.segment_sum(contrib, sorted_tok, num_segments=T)
    return out.reshape(Bt, L, D)

def layer(x, conv_prev, mk, mv, g_mix, w_in, g_v, w_s, b_s, w_conv, w_out,
          g_xattn, w_q, w_xo, g_moe, w_router, b_router, w1, b1, w2, b2):
    y, vrows, conv_new = mixer(rmsnorm(x, g_mix), conv_prev, w_in, g_v, w_s, b_s, w_conv, w_out)
    x = x + y
    x = x + cross_attn(rmsnorm(x, g_xattn), mk, mv, w_q, w_xo)
    x = x + moe(rmsnorm(x, g_moe), w_router, b_router, w1, b1, w2, b2)
    return x, vrows, conv_new

def setup_inputs(seed: int = 0) -> dict:
    key = jax.random.key(seed)
    ks = jax.random.split(key, 32)
    f32 = jnp.float32
    nrm = lambda k, shape, s: jax.random.normal(k, shape, f32) * s
    gain = lambda k, shape: 1.0 + 0.05 * jax.random.normal(k, shape, f32)
    return {
        "x_prompt": nrm(ks[0], (BATCH, SEQ, D_MODEL), 1.0),
        "x_sample": nrm(ks[1], (DEC_BATCH, DEC_SEQ, D_MODEL), 1.0),
        "mem_prompt": nrm(ks[2], (BATCH, N_MEM, D_MODEL), 1.0),
        "cache_mem_k": nrm(ks[3], (DEPTH, DEC_BATCH, N_MEM, X_HEADS, X_HEAD_DIM), 1.0),
        "cache_mem_v": nrm(ks[4], (DEPTH, DEC_BATCH, N_MEM, X_HEADS, X_HEAD_DIM), 1.0),
        "state_conv": nrm(ks[5], (DEPTH, DEC_BATCH, CONV_W - 1, B_WIDTH), 1.0),
        "g_mix": gain(ks[6], (DEPTH, D_MODEL)),
        "w_in": nrm(ks[7], (DEPTH, D_MODEL, IN_WIDTH), D_MODEL ** -0.5),
        "g_v": gain(ks[8], (DEPTH, A_HEADS, A_HEAD_DIM)),
        "w_spatial": nrm(ks[9], (DEPTH, A_HEADS, CHUNK, CHUNK), CHUNK ** -0.5),
        "b_spatial": gain(ks[10], (DEPTH, A_HEADS, CHUNK)),
        "w_conv": nrm(ks[11], (DEPTH, CONV_W, B_WIDTH), CONV_W ** -0.5),
        "w_out": nrm(ks[12], (DEPTH, MIX_WIDTH, D_MODEL), MIX_WIDTH ** -0.5),
        "g_xattn": gain(ks[13], (DEPTH, D_MODEL)),
        "g_mem": gain(ks[14], (DEPTH, D_MODEL)),
        "w_q": nrm(ks[15], (DEPTH, D_MODEL, D_MODEL), D_MODEL ** -0.5),
        "w_k": nrm(ks[16], (DEPTH, D_MODEL, D_MODEL), D_MODEL ** -0.5),
        "w_v": nrm(ks[17], (DEPTH, D_MODEL, D_MODEL), D_MODEL ** -0.5),
        "w_xo": nrm(ks[18], (DEPTH, D_MODEL, D_MODEL), D_MODEL ** -0.5),
        "g_moe": gain(ks[19], (DEPTH, D_MODEL)),
        "w_router": nrm(ks[20], (DEPTH, D_MODEL, N_EXPERTS), D_MODEL ** -0.5),
        "b_router": nrm(ks[21], (DEPTH, N_EXPERTS), 0.01),
        "w_gate_up": nrm(ks[22], (DEPTH, N_EXPERTS, D_MODEL, 2 * D_EXPERT), D_MODEL ** -0.5),
        "b_gate_up": nrm(ks[23], (DEPTH, N_EXPERTS, 2 * D_EXPERT), 0.02),
        "w_down": nrm(ks[24], (DEPTH, N_EXPERTS, D_EXPERT, D_MODEL), D_EXPERT ** -0.5),
        "b_down": nrm(ks[25], (DEPTH, N_EXPERTS, D_MODEL), 0.02),
        "g_final": gain(ks[26], (D_MODEL,)),
    }

def reference(x_prompt, x_sample, mem_prompt, cache_mem_k, cache_mem_v, state_conv,
              g_mix, w_in, g_v, w_spatial, b_spatial, w_conv, w_out,
              g_xattn, g_mem, w_q, w_k, w_v, w_xo,
              g_moe, w_router, b_router, w_gate_up, b_gate_up, w_down, b_down, g_final):
    xp = x_prompt
    xs = x_sample
    mk_p_list, mv_p_list, conv_p_list, conv_s_list, chunk_v_list = [], [], [], [], []
    for l in range(DEPTH):
        lw = (g_mix[l], w_in[l], g_v[l], w_spatial[l], b_spatial[l], w_conv[l], w_out[l],
              g_xattn[l], w_q[l], w_xo[l], g_moe[l], w_router[l], b_router[l],
              w_gate_up[l], b_gate_up[l], w_down[l], b_down[l])
        mk_p, mv_p = mem_kv(mem_prompt, g_mem[l], w_k[l], w_v[l])
        conv0 = jnp.zeros((xp.shape[0], CONV_W - 1, B_WIDTH), xp.dtype)
        xp, _, conv_p = layer(xp, conv0, mk_p, mv_p, *lw)
        xs, v_s, conv_s = layer(xs, state_conv[l], cache_mem_k[l], cache_mem_v[l], *lw)
        mk_p_list.append(mk_p)
        mv_p_list.append(mv_p)
        conv_p_list.append(conv_p)
        conv_s_list.append(conv_s)
        chunk_v_list.append(v_s)
    y_prompt = rmsnorm(xp, g_final)
    y_sample = rmsnorm(xs, g_final)
    mem_k_prompt = jnp.stack(mk_p_list)
    mem_v_prompt = jnp.stack(mv_p_list)
    conv_state_prompt = jnp.stack(conv_p_list)
    conv_state_sample = jnp.stack(conv_s_list)
    chunk_v_sample = jnp.stack(chunk_v_list)
    return (y_prompt, y_sample, mem_k_prompt, mem_v_prompt, conv_state_prompt, conv_state_sample, chunk_v_sample)


_drawn_inputs = setup_inputs


def setup_inputs(seed=0):
    import zlib

    import numpy as np

    out = dict(_drawn_inputs(seed))
    spreads = {}
    factors = {'g_xattn': 4.064, 'b_gate_up': 6.075, 'b_down': 7.036, 'b_router': 3.082}
    for name, (base, spread) in spreads.items():
        noise = np.random.default_rng([zlib.crc32(name.encode()), seed]).standard_normal(out[name].shape)
        drawn = base * np.exp(spread * noise) if base else spread * noise
        out[name] = __import__('jax').numpy.asarray(drawn.astype(out[name].dtype))
    for name, factor in factors.items():
        out[name] = (out[name] * factor).astype(out[name].dtype)
    return out
```

```python
from contextlib import ExitStack

import numpy as np
import concourse.bass as bass
from concourse import mybir
from concourse.alu_op_type import AluOpType as ALU

ACT = mybir.ActivationFunctionType
F32 = mybir.dt.float32
I32 = mybir.dt.int32
AX = mybir.AxisListType

P = 128
D = 1024
KT = D // P
NP_ = 256
NS = 8
T = NP_ + NS
TT = 3
NMEM = 256
HEADS = 4
NE = 32
TOPK = 4
SLOTS = 64
RING = 12
SLOT = 2048
EPS = 1e-5
LIMIT = 7.0
ALPHA = 1.702

PARAM_WIDTH = [("g_mix", 8), ("g_xattn", 8), ("g_mem", 8), ("g_moe", 8), ("g_final", 8), ("g_v", 4),
               ("w_conv", 12), ("w00", 4), ("state", 64), ("b_sp", 512), ("b_gu", 512), ("router", 256)]
PARAM_AT = {}
_at = 0
for _n, _w in PARAM_WIDTH:
    PARAM_AT[_n] = (_at, _at + _w)
    _at += _w
NPARAM = _at

IN_CHUNKS = [2, 3, 0, 1, 4, 5, 8, 9, 6, 7]
FRONT_CHUNKS = ([("w_k", c) for c in range(4)] + [("w_v", c) for c in range(4)]
                + [("w_in", c) for c in IN_CHUNKS] + [("w_out", c) for c in range(4)]
                + [("w_q", c) for c in range(4)] + [("kc", c) for c in range(NS)]
                + [("vc", c) for c in range(NS)] + [("w_xo", c) for c in range(4)])
NF = len(FRONT_CHUNKS)
CHUNK_AT = {key: n for n, key in enumerate(FRONT_CHUNKS)}

GROUPS = (["mem_ssq"] + [("k", m) for m in range(8)] + [("v", c, t) for c in range(4) for t in range(2)]
          + ["ssq0"] + [("in", m) for m in range(4, 8)] + [("in", m) for m in range(4)]
          + [("vssq", m) for m in range(4)] + [("in", m) for m in range(8, 12)]
          + [("vtok", c) for c in range(2)] + [("in", m) for m in range(16, 20)]
          + [("sg", m) for m in range(4)] + [("in", m) for m in range(12, 16)]
          + [("out", m) for m in range(8)] + ["ssq1"] + [("q", m) for m in range(8)]
          + [("s", t, h) for t in range(2) for h in range(2)] + ["sS"] + [("pT", h) for h in range(4)]
          + ["pST"] + [("o", m) for m in range(8)] + ["oS", "oST"] + [("xo", m) for m in range(8)]
          + ["ssq2", "lg", "lgT", "rank", "gT"] + [("htok", n) for n in range(6)]
          + [("ga", n) for n in range(4)] + [("bd", m) for m in range(8)])
G = {name: n for n, name in enumerate(GROUPS)}
NG = len(GROUPS)


def build(nc, x_t, mem_t, w_k, w_v, w_in, w_out, w_q, w_xo, kc, vc, w_gu, w_dn, params, ws_t,
          b_down, b_router, y_t, mk_t, mv, conv_p, conv_s, chunk_v):
    front_dram = {"w_k": w_k, "w_v": w_v, "w_in": w_in, "w_out": w_out, "w_q": w_q, "w_xo": w_xo,
                  "kc": kc, "vc": vc}
    with ExitStack() as ctx:
        def sb(name, shape, dt=F32):
            return ctx.enter_context(nc.sbuf_tensor(name, shape, dt))

        def sem(name):
            return ctx.enter_context(nc.semaphore(name))

        ring = sb("ring", [P, RING, SLOT])
        resid = sb("resid", [P, KT, T])
        par = sb("par", [P, NPARAM])
        ones = sb("ones", [P, P])
        ident = sb("ident", [P, P])
        before = sb("before", [P, P])
        blocks = sb("blocks", [P, P])
        slot_i = sb("slot_i", [P, SLOTS], I32)
        slot_no = sb("slot_no", [P, SLOTS])
        limit_i = sb("limit_i", [P, 4], I32)
        limits = sb("limits", [P, 4])
        sixty4 = sb("sixty4", [P, 4])
        valid = sb("valid", [P, TT])
        rstd = sb("rstd", [P, 2, T])
        rank = sb("rank", [P, TT, NE])
        gate = sb("gate", [P, TT, NE])
        brt = sb("brt", [NE, 1])
        iters = sb("iters", [1, 1], I32)
        arena = sb("arena", [P, 20700])

        def view(at, *shape):
            n = int(np.prod(shape))
            v = arena[:, at:at + n]
            if len(shape) == 2:
                v = v.rearrange("p (a b) -> p a b", a=shape[0])
            elif len(shape) == 3:
                v = v.rearrange("p (a b c) -> p a b c", a=shape[0], b=shape[1])
            elif len(shape) == 4:
                v = v.rearrange("p (a b c d) -> p a b c d", a=shape[0], b=shape[1], c=shape[2])
            return v

        proj = view(0, 20, T)
        q_fm = view(0, KT, T)
        o_fm = view(8 * T, KT, T)
        small = view(16 * T, 4 * T)
        at = 20 * T
        v_tok = view(at, 2, 512)
        ws = view(at + 1024, 8, P)
        probs = view(at, 2, 4, NMEM)
        at += 2048
        zp = view(at, 4, NP_ + 2)
        at += 4 * (NP_ + 2)
        zs = view(at, 4, 3, NS)
        at += 96
        conv = view(at, 4, T)
        at += 4 * T
        mem = view(at, KT, NMEM)
        q_diag = view(at, KT, NS, 32)
        at += 2048
        k_fm = view(at, KT, NMEM)
        probs_t = view(at, 4, 2, NP_)
        at += 2048
        v_mem = view(at, 2, D)
        at += 2048
        sq = view(at, KT, T)
        p_diag = view(at, NS, 2, HEADS, 32)
        sq_at = at
        at += KT * T
        p_flat = view(sq_at, NS * 2 * HEADS * 32)
        s_s = view(at, NMEM)
        s_st = view(at + 256, 2, P)
        o_s = view(at + 512, NMEM)
        at += 768
        h_fm = view(at, KT, T)
        h_at = at
        at += KT * T
        assert at <= 20700, at
        lT = small[0:NE, 0:384]
        lg = small[:, 384:480].rearrange("p (a b) -> p a b", a=TT)
        gt = small[:, 480:576].rearrange("p (a b) -> p a b", a=TT)
        eq = small[:, 576:672].rearrange("p (a b) -> p a b", a=TT)
        cum = small[:, 672:768].rearrange("p (a b) -> p a b", a=TT)
        ex = small[:, 768:864].rearrange("p (a b) -> p a b", a=TT)
        top8 = small[:, 864:888].rearrange("p (a b) -> p a b", a=TT)
        cnt3 = small[:, 888:891]
        gsum = small[:, 891:894]
        cmax = small[:, 894:895]
        over = small[:, 895:899]
        nover = small[:, 899:900]
        att_m = small[:, 900:910]
        att_s = small[:, 910:920]
        at = 20 * T
        h_tok = view(at, TT, D)
        at += TT * D
        p_hot = view(at, TT, 4 * SLOTS)
        at += TT * 4 * SLOTS
        w_hot = view(at, TT, 4 * SLOTS)
        at += TT * 4 * SLOTS
        xg = view(at, 2, KT, 4 * SLOTS)
        at += 2 * KT * 4 * SLOTS
        gu_sb = view(at, D)
        assert at + D <= sq_at
        y_hot = view(0, 2, D)
        tb = view(2 * D, KT, 2 * SLOTS)
        sig = view(3 * D, KT, SLOTS)
        hid = view(3 * D + KT * SLOTS, KT, SLOTS)
        assert 4 * D <= 16 * T
        g_hot = view(sq_at, 2, T)
        gate_t = view(sq_at + 2 * T, T)
        bdn = view(sq_at + 3 * T, D)
        assert 3 * T + D <= KT * T

        ps = ctx.enter_context(nc.psum_tensor("ps", [P, 8, 512], F32))

        def bank(name):
            return ps[:, G[name] % 8, :]

        def par_of(name):
            a, b = PARAM_AT[name]
            return par[:, a:b]

        g_v, w00 = par_of("g_v"), par_of("w00")
        w_conv = par_of("w_conv").rearrange("p (k m) -> p k m", k=3)
        state = par_of("state").rearrange("p (m k s) -> p m k s", m=4, k=2)
        b_sp = par_of("b_sp").rearrange("p (m t) -> p m t", m=4)
        b_gu = par_of("b_gu").rearrange("p (e h m) -> p e h m", e=NE, h=2)
        router = par_of("router").rearrange("p (k e) -> p k e", k=KT)

        mem_in, x_in, par_in, ws_in, brt_in, bdn_in = (
            sem(n) for n in ("mem_in", "x_in", "par_in", "ws_in", "brt_in", "bdn_in"))
        landed = [sem(f"landed{n}") for n in range(RING)]
        kv_stored = sem("kv_stored")
        mix_stored = sem("mix_stored")
        y_stored = sem("y_stored")
        grp = sem("grp")
        emptied = sem("emptied")
        kc_used = sem("kc_used")
        vc_used = sem("vc_used")
        const_ready = sem("const_ready")
        pool_step = sem("pool_step")
        dve_step = sem("dve_step")
        sq_ready = sem("sq_ready")
        std_ready = sem("std_ready")
        rstd_ready = sem("rstd_ready")
        h_ready = sem("h_ready")
        mem_ready = sem("mem_ready")
        v_act = sem("v_act")
        v_sq = sem("v_sq")
        v_std = sem("v_std")
        v_norm = sem("v_norm")
        u_act = sem("u_act")
        ws_masked = sem("ws_masked")
        z_zero = sem("z_zero")
        z_ready = sem("z_ready")
        a_ready = sem("a_ready")
        b_ready = sem("b_ready")
        qd_zero = sem("qd_zero")
        qd_ready = sem("qd_ready")
        pd_zero = sem("pd_zero")
        pd_ready = sem("pd_ready")
        s_exp = sem("s_exp")
        p_ready = sem("p_ready")
        os_ready = sem("os_ready")
        lt_zero = sem("lt_zero")
        ex_in = sem("ex_in")
        ex_out = sem("ex_out")
        sel_ready = sem("sel_ready")
        gate_ready = sem("gate_ready")
        rank_ready = sem("rank_ready")
        iters_ready = sem("iters_ready")
        h_norm = sem("h_norm")
        late_zero = sem("late_zero")
        p_built = sem("p_built")
        w_built = sem("w_built")
        rank_cut = sem("rank_cut")
        w_used = sem("w_used")
        gu_done = sem("gu_done")
        gu_copied = sem("gu_copied")
        t_done = sem("t_done")
        t_read = sem("t_read")
        g_ready = sem("g_ready")
        u_ready = sem("u_ready")
        ug_ready = sem("ug_ready")
        sig_ready = sem("sig_ready")
        hid_ready = sem("hid_ready")
        d_done = sem("d_done")
        y_copied = sem("y_copied")
        side_filled = sem("side_filled")
        side_copied = sem("side_copied")
        c_filled = sem("c_filled")
        c_added = sem("c_added")
        final_ssq = sem("final_ssq")
        final_var = sem("final_var")
        y_done = sem("y_done")

        block = ctx.enter_context(nc.Block())

        def front_free(eng, n):
            kind, c = FRONT_CHUNKS[n]
            if kind == "kc" and c < NS - 1:
                eng.wait_ge(kc_used, c + 1)
            elif kind == "vc" and c < NS - 1:
                eng.wait_ge(vc_used, c + 1)
            else:
                last = {"w_k": ("k", 2 * c + 1), "w_v": ("v", c, 1), "w_in": ("in", 2 * c + 1),
                        "w_out": ("out", 2 * c + 1), "w_q": ("q", 2 * c + 1), "w_xo": ("xo", 2 * c + 1),
                        "kc": "sS", "vc": "oS"}[kind]
                eng.wait_ge(grp, G[last] + 1)

        def front_uses(slot):
            return len(range(slot, NF, RING))

        def slot_of(c):
            return (NF + c) % RING

        def columns(t, first):
            quads = t[:].rearrange("p a (q c) -> p a q c", c=4)
            return quads[:, :, bass.ds(first, 1), :].rearrange("p a q c -> p a (q c)")

        def hot(t):
            return t[:].rearrange("p a (e s) -> p a e s", e=4)

        @block.sync
        def _(sp):
            sp.dma_start(mem[:], mem_t).then_inc(mem_in, 16)
            sp.dma_start(resid[:], x_t).then_inc(x_in, 16)
            for n, (kind, c) in enumerate(FRONT_CHUNKS):
                if n >= RING:
                    front_free(sp, n - RING)
                sp.dma_start(ring[:, n % RING, :], front_dram[kind][c]).then_inc(landed[n % RING], 16)

            def expert_chunk(e, c):
                dst = ring[:, slot_of(c), :]
                if c < 8:
                    src = w_gu[bass.ds(e, 1), c].rearrange("a p n -> (a p) n")
                else:
                    dst = dst.rearrange("p (k n) -> p k n", k=2)
                    src = w_dn[bass.ds(e, 1), 2 * (c - 8):2 * (c - 8) + 2].rearrange("a k p n -> p (a k) n")
                sp.dma_start(dst, src).then_inc(landed[slot_of(c)], 16)

            for c in range(RING):
                front_free(sp, NF - RING + c)
                expert_chunk(0, c)

            def expert_loads(e, expert):
                for c in range(RING):
                    if c == 7:
                        sp.wait_ge(gu_done, e)
                    elif c == 11:
                        sp.wait_ge(d_done, e)
                    else:
                        sp.wait_ge(w_used, e * 10 - 9 + (c if c < 7 else c - 1))
                    expert_chunk(expert, c)

            with sp.Fori(1, NE) as e:
                expert_loads(e, e)
            sp.wait_ge(iters_ready, 1)
            end = sp.value_load(iters[0:1, 0:1], min_val=4, max_val=20)
            with sp.If(end > 4):
                with sp.Fori(1, end >> 2) as again:
                    with sp.Fori(0, NE) as expert:
                        expert_loads(again * NE + expert, expert)
            sp.wait_ge(y_done, KT)
            sp.dma_start(y_t, resid[:]).then_inc(y_stored, 16)
            sp.wait_ge(y_stored, 16)
            sp.wait_ge(kv_stored, 32)
            sp.wait_ge(mix_stored, 48)

        @block.gpsimd
        def _(pool):
            counts = {}

            def step(ins, s=pool_step):
                counts[s.name] = counts.get(s.name, 0) + 1
                ins.then_inc(s, 1)
                pool.wait_ge(s, counts[s.name])

            step(nc.gpsimd.memset(ones[:], 1.0))
            step(nc.gpsimd.memset(ident[:], 0.0))
            step(nc.gpsimd.memset(blocks[:], 0.0))
            step(nc.gpsimd.memset(valid[:], 1.0))
            step(nc.gpsimd.affine_select(out=ident[:], in_=ident[:], compare_op=ALU.not_equal, fill=1.0, base=0,
                                    pattern=[[-1, P]], channel_multiplier=1), const_ready)
            step(nc.gpsimd.affine_select(out=before[:], in_=ones[:], compare_op=ALU.is_gt, fill=0.0, base=0,
                                    pattern=[[1, P]], channel_multiplier=-1), const_ready)
            step(nc.gpsimd.memset(blocks[0:64, 0:64], 1.0), const_ready)
            step(nc.gpsimd.memset(blocks[64:128, 64:128], 1.0), const_ready)
            step(nc.gpsimd.affine_select(out=valid[:, 2:3], in_=valid[:, 2:3], compare_op=ALU.is_ge, fill=0.0, base=NS - 1,
                                    pattern=[[0, 1]], channel_multiplier=-1), const_ready)
            step(nc.gpsimd.iota(slot_i[:], pattern=[[1, SLOTS]], base=0, channel_multiplier=0))
            step(nc.gpsimd.iota(limit_i[:], pattern=[[SLOTS, 4]], base=SLOTS, channel_multiplier=0))
            step(nc.gpsimd.tensor_copy(slot_no[:], slot_i[:]), const_ready)
            step(nc.gpsimd.tensor_copy(limits[:], limit_i[:]), const_ready)
            step(nc.gpsimd.memset(sixty4[:], float(SLOTS)), const_ready)
            step(nc.gpsimd.memset(zp[:, :, 0:2], 0.0), z_zero)
            pool.wait_ge(ws_in, 16)
            step(nc.gpsimd.affine_select(out=ws[:], in_=ws[:], compare_op=ALU.is_ge, fill=0.0, base=0,
                                    pattern=[[0, 8], [1, P]], channel_multiplier=-1), ws_masked)
            pool.wait_ge(grp, G[("v", 3, 1)] + 1)
            step(nc.gpsimd.memset(q_diag[:], 0.0), qd_zero)
            pool.wait_ge(grp, G["ssq1"] + 1)
            step(nc.gpsimd.memset(p_diag[:], 0.0), pd_zero)
            pool.wait_ge(grp, G[("out", 7)] + 1)
            step(nc.gpsimd.memset(lT, 0.0), lt_zero)
            pool.wait_ge(grp, G[("pT", 3)] + 1)
            pool.wait_ge(grp, G["oS"] + 1)
            pool.wait_ge(mix_stored, 48)
            step(nc.gpsimd.memset(h_tok[:, 2, :], 0.0), late_zero)
            pool.wait_ge(grp, G["ssq2"] + 1)
            step(nc.gpsimd.memset(gate_t[:], 0.0), late_zero)
            step(nc.gpsimd.memset(bdn[:], 0.0), late_zero)
            step(nc.gpsimd.memset(g_hot[:, 1, :], 0.0), late_zero)
            pool.wait_ge(grp, G[("xo", 7)] + 1)
            step(nc.gpsimd.memset(y_hot[:, 1, :], 0.0), late_zero)
            pool.wait_ge(rstd_ready, 4)
            pool.wait_ge(grp, G["lg"] + 1)
            step(nc.gpsimd.tensor_tensor(h_fm[:], h_fm[:], rstd[:, 1, :].unsqueeze(1).to_broadcast([P, KT, T]),
                                    ALU.mult), h_norm)

            def build_w(first, number):
                nc.gpsimd.tensor_tensor(hot(w_hot), hot(p_hot), columns(gate, first).unsqueeze(3).to_broadcast([P, TT, 4, SLOTS]),
                                        ALU.mult).then_inc(w_built, 1)
                pool.wait_ge(w_built, number)
                nc.gpsimd.tensor_tensor(columns(rank, first), columns(rank, first),
                                        sixty4[:].unsqueeze(1).to_broadcast([P, TT, 4]), ALU.subtract).then_inc(rank_cut, 1)
                pool.wait_ge(rank_cut, number)

            pool.wait_ge(rank_ready, 1)
            pool.wait_ge(gate_ready, 1)
            pool.wait_ge(p_built, 1)
            build_w(0, 1)
            pool.wait_ge(grp, G[("ga", 3)] + 1)
            pool.wait_ge(iters_ready, 1)
            end = pool.value_load(iters[0:1, 0:1], min_val=4, max_val=20)
            with pool.Fori(0, end) as it:
                for par_ in range(2):
                    quad = it * 2 + par_
                    first = (quad + 1) & 7
                    pool.wait_ge(side_filled, quad * 6 + 4 + 1)
                    pool.wait_ge(p_built, quad + 2)
                    build_w(first, quad + 2)

        @block.scalar
        def _(act):
            for credit in (gu_copied, y_copied, side_copied):
                act.sem_inc(credit, 1)
            act.dma_start(par[:], params).then_inc(par_in, 16)
            act.dma_start(ws[:], ws_t).then_inc(ws_in, 16)
            act.dma_start(brt[:], b_router).then_inc(brt_in, 16)

            def emptied_by(name):
                act.wait_ge(emptied, G[name] + 1)

            def root(name, v):
                emptied_by(name)
                nc.scalar.activation(v, v, ACT.Sqrt).then_inc(std_ready, 1)

            act.wait_ge(mem_in, 16)
            nc.scalar.activation(sq[:, :, 0:NMEM], mem[:], ACT.Square).then_inc(sq_ready, 1)
            root("mem_ssq", rstd[:, 0, 0:NMEM])
            act.wait_ge(x_in, 16)
            nc.scalar.activation(sq[:], resid[:], ACT.Square).then_inc(sq_ready, 1)
            emptied_by(("k", 7))
            act.dma_start(mk_t, k_fm[:]).then_inc(kv_stored, 16)
            emptied_by(("v", 3, 1))
            act.dma_start(mv, v_mem[:]).then_inc(kv_stored, 16)
            root("ssq0", rstd[:, 1, :])
            for m in range(4):
                emptied_by(("in", 4 + m))
                nc.scalar.activation(proj[:, 4 + m, :], proj[:, 4 + m, :], ACT.Gelu).then_inc(v_act, 1)
            for m in range(4):
                act.wait_ge(v_act, m + 1)
                nc.scalar.activation(sq[:, m, :], proj[:, 4 + m, :], ACT.Square).then_inc(v_sq, 1)
            for m in range(4):
                emptied_by(("in", m))
                nc.scalar.activation(proj[:, m, :], proj[:, m, :], ACT.Gelu).then_inc(u_act, 1)
            for m in range(4):
                emptied_by(("vssq", m))
                nc.scalar.activation(sq[:, 4 + m, :], sq[:, 4 + m, :], ACT.Sqrt).then_inc(v_std, 1)
            act.wait_ge(v_norm, 4)
            act.dma_start(chunk_v, proj[:, 4:8, NP_:T]).then_inc(mix_stored, 16)
            act.wait_ge(z_ready, 2)
            act.dma_start(conv_p, zp[:, :, NP_:NP_ + 2]).then_inc(mix_stored, 16)
            act.dma_start(conv_s, zs[:, :, 1:3, :]).then_inc(mix_stored, 16)
            for m in range(KT):
                emptied_by(("out", m))
                nc.scalar.activation(sq[:, m, :], resid[:, m, :], ACT.Square).then_inc(sq_ready, 1)
            root("ssq1", rstd[:, 0, :])
            for n in range(4):
                emptied_by(("s", n // 2, n % 2))
                v = probs[:, n // 2, 2 * (n % 2):2 * (n % 2) + 2, :]
                nc.scalar.activation(v, v, ACT.Exp, scale=1.0 / 16.0).then_inc(s_exp, 1)
            emptied_by("sS")
            nc.scalar.activation(s_s[:], s_s[:], ACT.Exp, scale=1.0 / 16.0).then_inc(s_exp, 1)
            act.wait_ge(grp, G["oS"] + 1)
            for m in range(KT):
                emptied_by(("xo", m))
                nc.scalar.activation(sq[:, m, :], resid[:, m, :], ACT.Square).then_inc(sq_ready, 1)
            root("ssq2", rstd[:, 1, :])
            act.wait_ge(ex_in, 1)
            nc.scalar.activation(ex[:], ex[:], ACT.Exp).then_inc(ex_out, 1)
            act.wait_ge(late_zero, 5)
            act.dma_start(bdn[0:NE, :], b_down).then_inc(bdn_in, 16)

            act.wait_ge(iters_ready, 1)
            end = act.value_load(iters[0:1, 0:1], min_val=4, max_val=20)
            act.wait_ge(emptied, NG)
            with act.Fori(0, end) as it:
                for j in range(8):
                    e, i, quad, nxt = it * 8 + j, j % 4, it * 2 + j // 4, (j // 4 + 1) % 2
                    act.wait_ge(gu_done, e + 1)
                    act.wait_ge(t_done, e + 1)
                    nc.scalar.activation(gu_sb.rearrange("p (a b) -> p a b", a=2), ps[:, 0:2, :],
                                         ACT.Copy).then_inc(gu_copied, 1)
                    pos = quad * 6 + (0, 2, 3, 5)[i]
                    if i % 2 == 0:
                        act.wait_ge(side_filled, pos + 2)
                        nc.scalar.activation(g_hot[:, i // 2, :], ps[:, 5, 0:T], ACT.Copy).then_inc(side_copied, 1)
                        pos = pos + 1
                    act.wait_ge(side_filled, pos + 2)
                    nc.scalar.activation(xg[:, nxt, 2 * i:2 * i + 2, :], ps[:, 5, :].rearrange("p (a b) -> p a b", a=2),
                                         ACT.Copy).then_inc(side_copied, 1)
                    act.wait_ge(g_ready, e + 1)
                    nc.scalar.activation(sig[:], tb[:, :, 0:SLOTS], ACT.Sigmoid, scale=ALPHA).then_inc(sig_ready, 1)
                    act.wait_ge(d_done, e + 1)
                    row = SLOTS * (i % 2)
                    nc.scalar.activation(y_hot[row:row + 64, i // 2, 0:512], ps[0:64, 4, :], ACT.Copy)
                    nc.scalar.activation(y_hot[row:row + 64, i // 2, 512:1024], ps[64:128, 4, :],
                                         ACT.Copy).then_inc(y_copied, 1)
            act.wait_ge(c_added, end * 32 + 8 + 1)
            nc.scalar.activation(h_fm[:], resid[:], ACT.Square).then_inc(sq_ready, 1)
            act.wait_ge(final_var, 1)
            nc.scalar.activation(rstd[:, 0, :], rstd[:, 0, :], ACT.Sqrt).then_inc(std_ready, 1)

        @block.vector
        def _(dve):
            for credit in (t_read, c_added):
                dve.sem_inc(credit, 1)
            TTN, TS, STT = nc.vector.tensor_tensor, nc.vector.tensor_scalar, nc.vector.scalar_tensor_tensor
            copy = nc.vector.tensor_copy
            steps = [0]

            def link(ins):
                steps[0] += 1
                ins.then_inc(dve_step, 1)
                dve.wait_ge(dve_step, steps[0])

            def filled(name, width=512):
                dve.wait_ge(grp, G[name] + 1)
                return bank(name)[:, 0:width]

            def bc(v, axis, shape):
                return v.unsqueeze(axis).to_broadcast(shape)

            def mean_square(name, v):
                TS(v, filled(name, v.shape[-1]), 1.0 / D, EPS, ALU.mult, ALU.add).then_inc(emptied, 1)

            def inverse(n, v):
                dve.wait_ge(std_ready, n)
                nc.vector.reciprocal(v, v).then_inc(rstd_ready, 1)
                dve.wait_ge(rstd_ready, n)

            def build_p(quad):
                slots = slot_no[:].unsqueeze(1).unsqueeze(1).to_broadcast([P, TT, 4, SLOTS])
                ranks = columns(rank, quad).unsqueeze(3).to_broadcast([P, TT, 4, SLOTS])
                TTN(hot(p_hot), slots, ranks, ALU.is_equal).then_inc(p_built, 1)

            dve.wait_ge(par_in, 16)
            mean_square("mem_ssq", rstd[:, 0, 0:NMEM])
            inverse(1, rstd[:, 0, 0:NMEM])
            for k in range(KT):
                STT(mem[:, k, :], mem[:, k, :], par_of("g_mem")[:, k:k + 1], rstd[:, 0, 0:NMEM],
                    ALU.mult, ALU.mult).then_inc(mem_ready, 1)
            dve.wait_ge(x_in, 16)
            for k in range(KT):
                TS(h_fm[:, k, :], resid[:, k, :], par_of("g_mix")[:, k:k + 1], None, ALU.mult).then_inc(h_ready, 1)
            for m in range(KT):
                copy(k_fm[:, m, :], filled(("k", m), NMEM)).then_inc(emptied, 1)
            for c in range(4):
                for t in range(2):
                    copy(v_mem[:, t, 256 * c:256 * c + 256], filled(("v", c, t), 256)).then_inc(emptied, 1)
            mean_square("ssq0", rstd[:, 1, :])
            inverse(2, rstd[:, 1, :])

            def projected(m, n=1):
                TTN(proj[:, m, :], filled(("in", m), T), rstd[:, n, :], ALU.mult).then_inc(emptied, 1)

            for m in range(4, 8):
                projected(m)
            for m in range(4):
                projected(m)
            for m in range(4):
                TS(sq[:, 4 + m, :], filled(("vssq", m), T), 1.0 / 64, EPS, ALU.mult, ALU.add).then_inc(emptied, 1)
            for m in range(4):
                dve.wait_ge(v_std, m + 1)
                link(nc.vector.reciprocal(sq[:, 4 + m, :], sq[:, 4 + m, :]))
                STT(proj[:, 4 + m, :], proj[:, 4 + m, :], g_v[:, m:m + 1], sq[:, 4 + m, :],
                    ALU.mult, ALU.mult).then_inc(v_norm, 1)
            for m in range(8, 12):
                projected(m)
            for c in range(2):
                copy(v_tok[:, c, :], filled(("vtok", c))).then_inc(emptied, 1)
            for m in range(16, 20):
                projected(m)
            dve.wait_ge(emptied, G[("in", 19)] + 1)
            TTN(zp[:, :, 2:], proj[:, 16:20, 0:NP_], proj[:, 8:12, 0:NP_], ALU.mult).then_inc(z_ready, 1)
            copy(zs[:, :, 0:2, :], state).then_inc(dve_step, 1)
            steps[0] += 1
            TTN(zs[:, :, 2, :], proj[:, 16:20, NP_:T], proj[:, 8:12, NP_:T], ALU.mult).then_inc(z_ready, 1)
            dve.wait_ge(z_ready, 2)
            dve.wait_ge(z_zero, 1)
            dve.wait_ge(u_act, 4)
            dve.wait_ge(v_norm, 4)
            for m in range(4):
                gated = conv[:, m, 0:NP_].rearrange("p (c t) -> p c t", c=2)
                TTN(gated, filled(("sg", m), NP_).rearrange("p (c t) -> p c t", c=2),
                    bc(b_sp[:, m, :], 1, [P, 2, P]), ALU.add).then_inc(emptied, 1)
                link(TS(conv[:, m, NP_:T], proj[:, 4 + m, NP_:T], w00[:, m:m + 1], b_sp[:, m, 0:1], ALU.mult, ALU.add))
                dve.wait_ge(emptied, G[("sg", m)] + 1)
                TTN(proj[:, m, :], proj[:, m, :], conv[:, m, :], ALU.mult).then_inc(a_ready, 1)
            dve.wait_ge(a_ready, 4)
            for m in range(4):
                TS(conv[:, m, 0:NP_], zp[:, m, 0:NP_], w_conv[:, 0, m:m + 1], None, ALU.mult)
                link(TS(conv[:, m, NP_:T], zs[:, m, 0, :], w_conv[:, 0, m:m + 1], None, ALU.mult))
            for k in range(1, 3):
                for m in range(4):
                    STT(conv[:, m, 0:NP_], zp[:, m, k:k + NP_], w_conv[:, k, m:m + 1], conv[:, m, 0:NP_], ALU.mult, ALU.add)
                    ins = STT(conv[:, m, NP_:T], zs[:, m, k, :], w_conv[:, k, m:m + 1], conv[:, m, NP_:T], ALU.mult, ALU.add)
                    ins.then_inc(dve_step, 1)
                    steps[0] += 1
                dve.wait_ge(dve_step, steps[0])
            for m in range(4):
                projected(12 + m)
                dve.wait_ge(emptied, G[("in", 12 + m)] + 1)
                TTN(proj[:, 12 + m, :], proj[:, 12 + m, :], conv[:, m, :], ALU.mult).then_inc(b_ready, 1)
            for m in range(KT):
                TTN(resid[:, m, :], resid[:, m, :], filled(("out", m), T), ALU.add).then_inc(emptied, 1)
                dve.wait_ge(emptied, G[("out", m)] + 1)
                TS(h_fm[:, m, :], resid[:, m, :], par_of("g_xattn")[:, m:m + 1], None, ALU.mult).then_inc(h_ready, 1)
            mean_square("ssq1", rstd[:, 0, :])
            inverse(3, rstd[:, 0, :])
            dve.wait_ge(mix_stored, 48)
            for m in range(KT):
                TTN(q_fm[:, m, :], filled(("q", m), T), rstd[:, 0, :], ALU.mult).then_inc(emptied, 1)
            dve.wait_ge(qd_zero, 1)
            dve.wait_ge(emptied, G[("q", 7)] + 1)
            diag = q_diag.rearrange("p k s c -> p k (s c)")[:, :, 0:(NS - 1) * 33 + 1:33]
            copy(diag, q_fm[:, :, NP_:T]).then_inc(qd_ready, 1)
            for n in range(4):
                name = ("s", n // 2, n % 2)
                b = filled(name).rearrange("p (h c) -> p h c", h=2)
                top = att_m[:, 2 * n:2 * n + 2]
                link(nc.vector.tensor_reduce(top, b, AX.X, ALU.max))
                TTN(probs[:, n // 2, 2 * (n % 2):2 * (n % 2) + 2, :], b, bc(top, 2, [P, 2, NMEM]),
                    ALU.subtract).then_inc(emptied, 1)
            link(nc.vector.tensor_reduce(att_m[:, 8:9], filled("sS", NMEM), AX.X, ALU.max))
            TS(s_s[:], filled("sS", NMEM), att_m[:, 8:9], None, ALU.subtract).then_inc(emptied, 1)
            for n in range(4):
                dve.wait_ge(s_exp, n + 1)
                v = probs[:, n // 2, 2 * (n % 2):2 * (n % 2) + 2, :]
                total = att_s[:, 2 * n:2 * n + 2]
                link(nc.vector.tensor_reduce(total, v, AX.X, ALU.add))
                link(nc.vector.reciprocal(total, total))
                TTN(v, v, bc(total, 2, [P, 2, NMEM]), ALU.mult).then_inc(p_ready, 1)
            dve.wait_ge(s_exp, 5)
            link(nc.vector.tensor_reduce(att_s[:, 8:9], s_s[:], AX.X, ALU.add))
            link(nc.vector.reciprocal(att_s[:, 8:9], att_s[:, 8:9]))
            TS(s_s[:], s_s[:], att_s[:, 8:9], None, ALU.mult).then_inc(p_ready, 1)
            dve.wait_ge(kv_stored, 32)
            for h in range(HEADS):
                copy(probs_t[:, h, :, :], filled(("pT", h)).rearrange("p (m q) -> p m q", m=2)).then_inc(emptied, 1)
            copy(s_st[:], filled("pST", 256).rearrange("p (m r) -> p m r", m=2)).then_inc(emptied, 1)
            dve.wait_ge(pd_zero, 1)
            dve.wait_ge(emptied, G["pST"] + 1)
            for mt in range(2):
                for h in range(HEADS):
                    flat = p_flat[:, (mt * HEADS + h) * 32:(mt * HEADS + h) * 32 + (NS - 1) * 257 + 1:257]
                    copy(flat, s_st[:, mt, 32 * h:32 * h + NS]).then_inc(pd_ready, 1)
            for m in range(KT):
                copy(o_fm[:, m, 0:NP_], filled(("o", m), NP_)).then_inc(emptied, 1)
            copy(o_s[:], filled("oS", NMEM)).then_inc(emptied, 1)
            b = filled("oST", 256).rearrange("p (k h c) -> p h k c", k=2, h=HEADS)
            o_heads = o_fm.rearrange("p (h k) t -> p h k t", h=HEADS)
            for k in range(2):
                ins = copy(o_heads[:, :, k, NP_:T], b[:, :, k, 0:NS])
                ins.then_inc(os_ready if k == 0 else emptied, 1)
            for m in range(KT):
                TTN(resid[:, m, :], resid[:, m, :], filled(("xo", m), T), ALU.add).then_inc(emptied, 1)
                dve.wait_ge(emptied, G[("xo", m)] + 1)
                TS(h_fm[:, m, :], resid[:, m, :], par_of("g_moe")[:, m:m + 1], None, ALU.mult).then_inc(h_ready, 1)
            mean_square("ssq2", rstd[:, 1, :])
            inverse(4, rstd[:, 1, :])
            dve.wait_ge(brt_in, 16)
            dve.wait_ge(lt_zero, 1)
            link(TTN(lT[:, 0:T], filled("lg", T)[0:NE], rstd[0:NE, 1, :], ALU.mult))
            TS(lT[:, 0:T], lT[:, 0:T], brt[:, 0:1], None, ALU.add).then_inc(emptied, 1)
            copy(lg[:], filled("lgT", 96).rearrange("p (a e) -> p a e", a=TT)).then_inc(emptied, 1)
            dve.wait_ge(emptied, G["lgT"] + 1)
            for t in range(TT):
                link(nc.vector.max(top8[:, t, :], lg[:, t, :]))
            TTN(ex[:], lg[:], top8[:, :, 0:1].to_broadcast([P, TT, NE]), ALU.subtract).then_inc(ex_in, 1)
            fourth = top8[:, :, TOPK - 1:TOPK].to_broadcast([P, TT, NE])
            link(TTN(gt[:], lg[:], fourth, ALU.is_gt))
            link(TTN(eq[:], lg[:], fourth, ALU.is_equal))
            link(nc.vector.tensor_reduce(cnt3, gt[:], AX.X, ALU.add))
            link(TS(cnt3, cnt3, -1.0, float(TOPK), ALU.mult, ALU.add))
            for t in range(TT):
                link(nc.vector.tensor_tensor_scan(cum[:, t, :], ones[:, 0:NE], eq[:, t, :], 0.0, ALU.mult, ALU.add))
            link(TTN(cum[:], cum[:], bc(cnt3, 2, [P, TT, NE]), ALU.is_le))
            link(TTN(eq[:], eq[:], cum[:], ALU.mult))
            link(TTN(gt[:], gt[:], eq[:], ALU.add))
            dve.wait_ge(ex_out, 1)
            link(TTN(ex[:], ex[:], gt[:], ALU.mult))
            TTN(gt[:], gt[:], bc(valid[:], 2, [P, TT, NE]), ALU.mult).then_inc(sel_ready, 1)
            link(nc.vector.tensor_reduce(gsum, ex[:], AX.X, ALU.add))
            link(nc.vector.reciprocal(gsum, gsum))
            link(TTN(gsum, gsum, valid[:], ALU.mult))
            TTN(gate[:], ex[:], bc(gsum, 2, [P, TT, NE]), ALU.mult).then_inc(gate_ready, 1)
            dve.wait_ge(sel_ready, 1)
            b = filled("rank", 128)
            link(nc.vector.tensor_reduce(cmax, b[:, 96:128], AX.X, ALU.max))
            STT(rank[:], b[:, 0:96].rearrange("p (a e) -> p a e", a=TT), 1.0, gt[:], ALU.add, ALU.mult).then_inc(emptied, 1)
            dve.wait_ge(emptied, G["rank"] + 1)
            TS(rank[:], rank[:], -1.0, None, ALU.add).then_inc(rank_ready, 1)
            link(TTN(over, limits[:], cmax.to_broadcast([P, 4]), ALU.is_lt))
            link(nc.vector.tensor_reduce(nover, over, AX.X, ALU.add))
            TS(iters[:], nover[0:1, :], 4.0, 4.0, ALU.mult, ALU.add).then_inc(iters_ready, 1)
            dve.wait_ge(late_zero, 5)
            for t in range(TT):
                width = P if t < 2 else NS
                ins = copy(gate_t[0:NE, P * t:P * t + width], filled("gT", 384)[0:NE, P * t:P * t + width])
                ins.then_inc(dve_step if t < 2 else emptied, 1)
            steps[0] += 2
            for n in range(6):
                rows = P if n < 4 else NS
                copy(h_tok[0:rows, n // 2, 512 * (n % 2):512 * (n % 2) + 512],
                     filled(("htok", n))[0:rows]).then_inc(emptied, 1)
            dve.wait_ge(rank_ready, 1)
            build_p(0)
            for n in range(4):
                copy(xg[:, 0, 2 * n:2 * n + 2, :], filled(("ga", n)).rearrange("p (a b) -> p a b", a=2)).then_inc(emptied, 1)
            for m in range(KT):
                TTN(resid[:, m, :], resid[:, m, :], filled(("bd", m), T), ALU.add).then_inc(emptied, 1)
            dve.wait_ge(emptied, NG)

            def combine(n, m):
                dve.wait_ge(c_filled, n + 1)
                TTN(resid[:, m, :], resid[:, m, :], ps[:, 6 + m % 2, 0:T], ALU.add).then_inc(c_added, 1)

            dve.wait_ge(iters_ready, 1)
            end = dve.value_load(iters[0:1, 0:1], min_val=4, max_val=20)
            with dve.Fori(0, end) as it:
                expert0 = (it & 3) * 8
                for j in range(8):
                    e, i, quad = it * 8 + j, j % 4, it * 2 + j // 4
                    if i == 0:
                        dve.wait_ge(side_filled, quad * 6 + 1)
                        dve.wait_ge(rank_cut, quad + 1)
                        build_p((quad + 1) & 7)
                    dve.wait_ge(c_added, e * 4 + 1)
                    for r in range(2):
                        combine(e * 4 + r, 4 * (i % 2) + r)
                    dve.wait_ge(t_done, e + 2)
                    turned = ps[:, 2:4, :].rearrange("p a (k h s) -> p (a k) h s", h=2, s=SLOTS)
                    both = tb.rearrange("p k (h s) -> p k h s", h=2)
                    for h in range(2):
                        bias = b_gu[:, bass.ds(expert0 + j, 1), h, :].rearrange("p a m -> p (a m)")
                        TTN(both[:, :, h, :], turned[:, :, h, :], bc(bias, 2, [P, KT, SLOTS]),
                            ALU.add).then_inc(t_read, 1)
                    gate_v, up_v = tb[:, :, 0:SLOTS], tb[:, :, SLOTS:2 * SLOTS]
                    dve.wait_ge(t_read, e * 2 + 3)
                    TS(gate_v, gate_v, LIMIT, None, ALU.min).then_inc(g_ready, 1)
                    TS(up_v, up_v, LIMIT, -LIMIT, ALU.min, ALU.max).then_inc(u_ready, 1)
                    dve.wait_ge(u_ready, e + 1)
                    dve.wait_ge(g_ready, e + 1)
                    STT(up_v, up_v, 1.0, gate_v, ALU.add, ALU.mult).then_inc(ug_ready, 1)
                    for r in range(2, 4):
                        combine(e * 4 + r, 4 * (i % 2) + r)
                    dve.wait_ge(sig_ready, e + 1)
                    dve.wait_ge(ug_ready, e + 1)
                    TTN(hid[:], up_v, sig[:], ALU.mult).then_inc(hid_ready, 1)
            dve.wait_ge(c_added, end * 32 + 1)
            for m in range(KT):
                combine(end * 32 + m, m)
            dve.wait_ge(final_ssq, 1)
            TS(rstd[:, 0, :], ps[:, 0, 0:T], 1.0 / D, EPS, ALU.mult, ALU.add).then_inc(final_var, 1)
            inverse(5, rstd[:, 0, :])
            dve.wait_ge(c_added, end * 32 + 8 + 1)
            for m in range(KT):
                STT(resid[:, m, :], resid[:, m, :], par_of("g_final")[:, m:m + 1], rstd[:, 0, :],
                    ALU.mult, ALU.mult).then_inc(y_done, 1)

        @block.tensor
        def _(pe):
            for credit in (t_done, side_filled):
                pe.sem_inc(credit, 1)
            mm, turn = nc.tensor.matmul, nc.tensor.transpose

            def begin(name):
                if G[name] >= 8:
                    pe.wait_ge(emptied, G[name] - 7)
                return bank(name)

            def chunk(key):
                n = CHUNK_AT[key]
                pe.wait_ge(landed[n % RING], 16 * (n // RING + 1))
                return ring[:, n % RING, :]

            def sum_squares(name, width, waits):
                b = begin(name)
                for k in range(KT):
                    pe.wait_ge(sq_ready, waits(k))
                    last = mm(b[:, 0:width], ones[:], sq[:, k, 0:width], start=(k == 0), stop=(k == KT - 1))
                last.then_inc(grp, 1)

            def project(kind, m, source, c=None):
                w = chunk((kind, m // 2)).rearrange("p (k n) -> p k n", k=KT)
                b = begin((kind if c is None else c, m))
                src = source(0)
                width = src.shape[-1]
                for k in range(KT):
                    last = mm(b[:, 0:width], w[:, k, P * (m % 2):P * (m % 2) + P], source(k),
                              start=(k == 0), stop=(k == KT - 1))
                last.then_inc(grp, 1)

            pe.wait_ge(const_ready, 8)
            sum_squares("mem_ssq", NMEM, lambda k: 1)
            pe.wait_ge(mem_ready, 8)
            for m in range(KT):
                project("w_k", m, lambda k: mem[:, k, :], "k")
            for c in range(4):
                w = chunk(("w_v", c)).rearrange("p (k n) -> p k n", k=KT)
                for t in range(2):
                    b = begin(("v", c, t))
                    for k in range(KT):
                        last = mm(b[:, 0:256], mem[:, k, P * t:P * t + P], w[:, k, :], start=(k == 0), stop=(k == KT - 1))
                    last.then_inc(grp, 1)
            sum_squares("ssq0", T, lambda k: 2)
            pe.wait_ge(h_ready, KT)

            def gained(k):
                return h_fm[:, k, :]

            for m in (4, 5, 6, 7, 0, 1, 2, 3):
                project("w_in", m, gained, "in")
            for m in range(4):
                b = begin(("vssq", m))
                pe.wait_ge(v_sq, m + 1)
                mm(b[:, 0:T], blocks[:], sq[:, m, :], start=True, stop=True).then_inc(grp, 1)
            for m in range(8, 12):
                project("w_in", m, gained, "in")
            for c in range(2):
                b = begin(("vtok", c))
                for m in range(4):
                    pe.wait_ge(v_norm, m + 1)
                    last = turn(b[:, P * m:P * m + P], proj[:, 4 + m, P * c:P * c + P], ident[:])
                last.then_inc(grp, 1)
            for m in range(16, 20):
                project("w_in", m, gained, "in")
            pe.wait_ge(ws_masked, 1)
            pe.wait_ge(emptied, G[("vtok", 1)] + 1)
            for m in range(4):
                b = begin(("sg", m))
                for c in range(2):
                    for hh in range(2):
                        head = 2 * m + hh
                        last = mm(b[64 * hh:64 * hh + 64, P * c:P * c + P], v_tok[:, c, 64 * head:64 * head + 64],
                                  ws[:, head, :], start=True, stop=True)
                last.then_inc(grp, 1)
            for m in range(12, 16):
                project("w_in", m, gained, "in")

            def mixed(k):
                return proj[:, k if k < 4 else 8 + k, :]

            pe.wait_ge(a_ready, 4)
            pe.wait_ge(b_ready, 4)
            for m in range(KT):
                project("w_out", m, mixed, "out")
            sum_squares("ssq1", T, lambda k: 3 + k)
            pe.wait_ge(h_ready, 2 * KT)
            for m in range(KT):
                project("w_q", m, gained, "q")
            pe.wait_ge(emptied, G[("q", 7)] + 1)
            for t in range(2):
                for pair in range(2):
                    b = begin(("s", t, pair))
                    for hh in range(2):
                        for dk in range(2):
                            ft = 2 * (2 * pair + hh) + dk
                            last = mm(b[:, NMEM * hh:NMEM * hh + NMEM], q_fm[:, ft, P * t:P * t + P], k_fm[:, ft, :],
                                      start=(dk == 0), stop=(dk == 1))
                    last.then_inc(grp, 1)
            b = begin("sS")
            pe.wait_ge(qd_ready, 1)
            for t in range(NS):
                keys = chunk(("kc", t)).rearrange("p (k n) -> p k n", k=KT)
                for dk in range(2):
                    for h in range(HEADS):
                        last = mm(b[32 * h:32 * h + 32, 0:NMEM], q_diag[:, 2 * h + dk, t, :], keys[:, 2 * h + dk, :],
                                  start=(t == 0 and dk == 0), stop=(t == NS - 1 and dk == 1),
                                  tile_position=(0, 32 * h))
                last.then_inc(kc_used if t < NS - 1 else grp, 1)
            for h in range(HEADS):
                b = begin(("pT", h))
                for mt in range(2):
                    for t in range(2):
                        pe.wait_ge(p_ready, 2 * t + h // 2 + 1)
                        last = turn(b[:, 256 * mt + P * t:256 * mt + P * t + P], probs[:, t, h, P * mt:P * mt + P], ident[:])
                last.then_inc(grp, 1)
            b = begin("pST")
            pe.wait_ge(p_ready, 5)
            for mt in range(2):
                last = turn(b[:, P * mt:P * mt + P], s_s[:, P * mt:P * mt + P], ident[:])
            last.then_inc(grp, 1)
            for m in range(KT):
                b = begin(("o", m))
                pe.wait_ge(emptied, G[("pT", m // 2)] + 1)
                for mt in range(2):
                    last = mm(b[:, 0:NP_], v_mem[:, mt, P * m:P * m + P], probs_t[:, m // 2, mt, :],
                              start=(mt == 0), stop=(mt == 1))
                last.then_inc(grp, 1)
            b = begin("oS")
            pe.wait_ge(pd_ready, 8)
            for t in range(NS):
                values = chunk(("vc", t)).rearrange("p (m n) -> p m n", m=2)
                for mt in range(2):
                    for h in range(HEADS):
                        last = mm(b[32 * h:32 * h + 32, 0:256], p_diag[:, t, mt, h, :], values[:, mt, 256 * h:256 * h + 256],
                                  start=(t == 0 and mt == 0), stop=(t == NS - 1 and mt == 1),
                                  tile_position=(0, 32 * h))
                last.then_inc(vc_used if t < NS - 1 else grp, 1)
            b = begin("oST")
            pe.wait_ge(emptied, G["oS"] + 1)
            for dk in range(2):
                last = turn(b[:, P * dk:P * dk + P], o_s[:, P * dk:P * dk + P], ident[:])
            last.then_inc(grp, 1)
            pe.wait_ge(emptied, G["oST"] + 1)
            pe.wait_ge(os_ready, 1)
            for m in range(KT):
                project("w_xo", m, lambda k: o_fm[:, k, :], "xo")
            sum_squares("ssq2", T, lambda k: 11 + k)
            b = begin("lg")
            pe.wait_ge(h_ready, 3 * KT)
            for k in range(KT):
                last = mm(b[0:NE, 0:T], router[:, k, :], h_fm[:, k, :], start=(k == 0), stop=(k == KT - 1))
            last.then_inc(grp, 1)
            b = begin("lgT")
            pe.wait_ge(emptied, G["lg"] + 1)
            for t in range(TT):
                last = turn(b[:, NE * t:NE * t + NE], lT[:, P * t:P * t + P], ident[0:NE, 0:NE])
            last.then_inc(grp, 1)
            b = begin("rank")
            pe.wait_ge(sel_ready, 1)
            for t in range(TT):
                for s in range(t + 1):
                    mm(b[:, NE * t:NE * t + NE], before[:] if s == t else ones[:], gt[:, s, :], start=(s == 0), stop=(s == t))
            for s in range(TT):
                last = mm(b[:, 96:128], ones[:], gt[:, s, :], start=(s == 0), stop=(s == TT - 1))
            last.then_inc(grp, 1)
            b = begin("gT")
            pe.wait_ge(gate_ready, 1)
            for t in range(TT):
                last = turn(b[0:NE, P * t:P * t + P], gate[:, t, :], ident[:])
            last.then_inc(grp, 1)
            pe.wait_ge(h_norm, 1)
            for n in range(6):
                b = begin(("htok", n))
                width = P if n < 4 else NS
                for f in range(4):
                    last = turn(b[0:width, P * f:P * f + P],
                                h_fm[:, 4 * (n % 2) + f, P * (n // 2):P * (n // 2) + width], ident[:])
                last.then_inc(grp, 1)

            def gather(b, n):
                for half in range(2):
                    f = 2 * n + half
                    for t in range(TT):
                        last = mm(b[:, 256 * half:256 * half + 256], h_tok[:, t, P * f:P * f + P], p_hot[:, t, :],
                                  start=(t == 0), stop=(t == TT - 1))
                return last

            pe.wait_ge(p_built, 1)
            pe.wait_ge(late_zero, 5)
            pe.wait_ge(emptied, G[("htok", 5)] + 1)
            for n in range(4):
                gather(begin(("ga", n)), n).then_inc(grp, 1)
            pe.wait_ge(bdn_in, 16)
            pe.wait_ge(emptied, G["gT"] + 1)
            for m in range(KT):
                b = begin(("bd", m))
                mm(b[:, 0:T], bdn[:, P * m:P * m + P], gate_t[:], start=True, stop=True).then_inc(grp, 1)
            pe.wait_ge(emptied, NG)

            def combine(n, r, m, pair):
                if r == 0:
                    pe.wait_ge(c_added, n + 1)
                elif r >= 2:
                    pe.wait_ge(c_added, n + r - 1 + 1)
                mm(ps[:, 6 + m % 2, 0:T], y_hot[:, pair, P * m:P * m + P], g_hot[:, pair, :],
                   start=True, stop=True).then_inc(c_filled, 1)

            pe.wait_ge(iters_ready, 1)
            end = pe.value_load(iters[0:1, 0:1], min_val=4, max_val=20)
            with pe.Fori(0, end) as it:
                for j in range(8):
                    e, i, cur = it * 8 + j, j % 4, j // 4
                    quad = it * 2 + cur

                    def expert_chunk(c):
                        s = slot_of(c)
                        pe.wait_ge(landed[s], e * 16 + 16 * (front_uses(s) + 1))
                        return ring[:, s, :]

                    pe.wait_ge(gu_copied, e + 1)
                    if i == 0:
                        pe.wait_ge(side_copied, quad * 6 + 1)
                    for k in range(KT):
                        w = expert_chunk(k)
                        for n in range(2):
                            for h in range(2):
                                last = mm(ps[64 * h:64 * h + 64, n, :], xg[:, cur, k, SLOTS * i:SLOTS * i + SLOTS],
                                          w[:, D * h + 512 * n:D * h + 512 * n + 512], start=(k == 0), stop=(k == KT - 1))
                        last.then_inc(w_used if k < KT - 1 else gu_done, 1)
                    pos = quad * 6 + (0, 2, 3, 5)[i]
                    if i % 2 == 0:
                        pe.wait_ge(side_copied, pos + 1)
                        pe.wait_ge(w_built, quad + 1)
                        for t in range(TT):
                            width = P if t < 2 else NS
                            last = turn(ps[:, 5, P * t:P * t + width], w_hot[0:width, t, P * (i // 2):P * (i // 2) + P],
                                        ident[0:width, 0:width])
                        last.then_inc(side_filled, 1)
                        pos = pos + 1
                    pair = 1 - i // 2
                    if i == 0:
                        pe.wait_ge(y_copied, quad * 4 + 1)
                    if i == 2:
                        pe.wait_ge(y_copied, quad * 4 + 3)
                    for r in range(2):
                        combine(e * 4, r, 4 * (i % 2) + r, pair)
                    pe.wait_ge(side_copied, pos + 1)
                    pe.wait_ge(p_built, quad + 2)
                    gather(ps[:, 5, :], i).then_inc(side_filled, 1)
                    pe.wait_ge(gu_copied, e + 2)
                    pe.wait_ge(t_read, e * 2 + 1)
                    for f in range(KT):
                        last = turn(ps[:, 2 + f // 4, P * (f % 4):P * (f % 4) + P], gu_sb[:, P * f:P * f + P], ident[:])
                    last.then_inc(t_done, 1)
                    for r in range(2, 4):
                        combine(e * 4, r, 4 * (i % 2) + r, pair)
                    pe.wait_ge(hid_ready, e + 1)
                    pe.wait_ge(y_copied, e + 1)
                    for c in range(8, RING):
                        w = expert_chunk(c)
                        for kk in range(2):
                            k = 2 * (c - 8) + kk
                            for h in range(2):
                                last = mm(ps[64 * h:64 * h + 64, 4, :], hid[:, k, :],
                                          w[:, D * kk + 512 * h:D * kk + 512 * h + 512], start=(k == 0), stop=(k == KT - 1))
                        last.then_inc(w_used if c < RING - 1 else d_done, 1)
            pe.wait_ge(y_copied, end * 8 + 1)
            for m in range(KT):
                pe.wait_ge(c_added, end * 32 + max(m - 1, 0) + 1)
                mm(ps[:, 6 + m % 2, 0:T], y_hot[:, 1, P * m:P * m + P], g_hot[:, 1, :],
                   start=True, stop=True).then_inc(c_filled, 1)
            pe.wait_ge(sq_ready, 19)
            for k in range(KT):
                last = mm(ps[:, 0, 0:T], ones[:], h_fm[:, k, :], start=(k == 0), stop=(k == KT - 1))
            last.then_inc(final_ssq, 1)


def feature_major(a):
    return np.ascontiguousarray(a.reshape(a.shape[0], -1, P).transpose(2, 1, 0))


def weight_chunks(w):
    k, n = w.shape[0] // P, w.shape[1] // 256
    return np.ascontiguousarray(w.reshape(k, P, n, 256).transpose(2, 1, 0, 3)).reshape(n, P, k * 256)


def kernel(**inputs):
    import concourse.bacc as bacc
    from concourse.bass_utils import run_bass_kernel_spmd

    a = {k: np.asarray(v) for k, v in inputs.items()}
    vec = lambda v: v.reshape(-1, P).T
    heads = lambda v: np.repeat(v, 64, axis=0)
    small = {
        "g_mix": vec(a["g_mix"]), "g_xattn": vec(a["g_xattn"]), "g_mem": vec(a["g_mem"]), "g_moe": vec(a["g_moe"]),
        "g_final": vec(a["g_final"]), "g_v": vec(a["g_v"]), "w_conv": vec(a["w_conv"]),
        "w00": vec(heads(a["w_spatial"][0, :, 0, 0])),
        "state": a["state_conv"][0].reshape(NS, 2, 4, P).transpose(3, 2, 1, 0).reshape(P, 64),
        "b_sp": heads(a["b_spatial"][0]).reshape(4, P, P).transpose(1, 0, 2).reshape(P, 512),
        "b_gu": a["b_gate_up"][0].reshape(NE, 16, P).transpose(2, 0, 1).reshape(P, 512),
        "router": a["w_router"][0].reshape(KT, P, NE).transpose(1, 0, 2).reshape(P, 256),
    }
    x = np.concatenate([a["x_prompt"][0], a["x_sample"][:, 0]], axis=0)
    kc = a["cache_mem_k"][0].reshape(NS, NMEM, KT, P).transpose(0, 3, 2, 1).reshape(NS, P, SLOT)
    vc = a["cache_mem_v"][0].reshape(NS, 2, P, D).transpose(0, 2, 1, 3).reshape(NS, P, SLOT)
    arrays = {
        "x_t": feature_major(x), "mem_t": feature_major(a["mem_prompt"][0]),
        "w_k": weight_chunks(a["w_k"][0]), "w_v": weight_chunks(a["w_v"][0]), "w_in": weight_chunks(a["w_in"][0]),
        "w_out": weight_chunks(a["w_out"][0]), "w_q": weight_chunks(a["w_q"][0]), "w_xo": weight_chunks(a["w_xo"][0]),
        "kc": np.ascontiguousarray(kc), "vc": np.ascontiguousarray(vc),
        "w_gu": a["w_gate_up"][0].reshape(NE, KT, P, 2 * D), "w_dn": a["w_down"][0].reshape(NE, KT, P, D),
        "params": np.ascontiguousarray(np.concatenate([small[n] for n, _ in PARAM_WIDTH], axis=1)),
        "ws_t": np.ascontiguousarray(a["w_spatial"][0].transpose(2, 0, 1)),
        "b_down": a["b_down"][0], "b_router": a["b_router"].reshape(NE, 1),
    }
    outs = {"y_t": (P, KT, T), "mk_t": (P, KT, NMEM), "mv": (P, 2, D), "conv_p": (P, 4, 2),
            "conv_s": (P, 4, 2, NS), "chunk_v": (P, 4, NS)}
    nc = bacc.Bacc("TRN2", target_bir_lowering=False, num_devices=1)
    args, given = [], {}
    for name, v in arrays.items():
        given[f"in_{name}"] = np.ascontiguousarray(v)
        args.append(nc.dram_tensor(f"in_{name}", v.shape, F32, kind="ExternalInput").ap())
    for name, shape in outs.items():
        args.append(nc.dram_tensor(f"out_{name}", shape, F32, kind="ExternalOutput").ap())
    build(nc, *args)
    got = run_bass_kernel_spmd(nc, [given], core_ids=[0]).results[0]
    y = got["out_y_t"].transpose(2, 1, 0).reshape(T, D)
    mk = got["out_mk_t"].transpose(2, 1, 0).reshape(1, 1, NMEM, HEADS, NMEM)
    v_m = got["out_mv"].transpose(1, 0, 2).reshape(1, 1, NMEM, HEADS, NMEM)
    conv_p = got["out_conv_p"].transpose(2, 1, 0).reshape(1, 1, 2, 512)
    conv_s = got["out_conv_s"].transpose(3, 2, 1, 0).reshape(1, NS, 2, 512)
    chunk_v = got["out_chunk_v"].transpose(2, 1, 0).reshape(1, NS, 1, 8, 64)
    return (np.ascontiguousarray(y[:NP_]).reshape(1, NP_, D), np.ascontiguousarray(y[NP_:]).reshape(NS, 1, D),
            np.ascontiguousarray(mk), np.ascontiguousarray(v_m), np.ascontiguousarray(conv_p),
            np.ascontiguousarray(conv_s), np.ascontiguousarray(chunk_v))
```

```python
from contextlib import ExitStack

import numpy as np
import concourse.bass as bass
from concourse import mybir
from concourse.alu_op_type import AluOpType as ALU

ACT = mybir.ActivationFunctionType
F32 = mybir.dt.float32
I32 = mybir.dt.int32
AX = mybir.AxisListType

P = 128
D = 1024
KT = D // P
NP_ = 256
NS = 8
T = NP_ + NS
TT = 3
NMEM = 256
HEADS = 4
NE = 32
TOPK = 4
SLOTS = 64
RING = 12
SLOT = 2048
EPS = 1e-5
LIMIT = 7.0
ALPHA = 1.702

PARAM_WIDTH = [("g_mix", 8), ("g_xattn", 8), ("g_mem", 8), ("g_moe", 8), ("g_final", 8), ("g_v", 4),
               ("w_conv", 12), ("w00", 4), ("state", 64), ("b_sp", 512), ("router", 256), ("b_router", 32),
               ("b_gu", 512)]
PARAM_AT = {}
_at = 0
for _n, _w in PARAM_WIDTH:
    PARAM_AT[_n] = (_at, _at + _w)
    _at += _w
NPARAM = _at
NGAIN = PARAM_AT["g_v"][0]

IN_CHUNKS = [2, 3, 0, 1, 4, 5, 8, 9, 6, 7]
FRONT_CHUNKS = ([("w_k", c) for c in range(4)] + [("w_v", c) for c in range(4)]
                + [("w_in", c) for c in IN_CHUNKS] + [("w_out", c) for c in range(4)]
                + [("w_q", c) for c in range(4)] + [("kc", c) for c in range(NS)]
                + [("vc", c) for c in range(NS)] + [("w_xo", c) for c in range(4)])
NF = len(FRONT_CHUNKS)
CHUNK_AT = {key: n for n, key in enumerate(FRONT_CHUNKS)}

GROUPS = ([("k", 0), ("k", 1), "mem_ssq"] + [("k", m) for m in range(2, 8)]
          + [("v", 0, t) for t in range(2)] + ["ssq0"] + [("v", c, t) for c in range(1, 4) for t in range(2)] + [("in", m) for m in range(4, 8)] + [("in", m) for m in range(4)]
          + [("vssq", m) for m in range(4)] + [("in", m) for m in range(8, 12)]
          + [("vtok", c) for c in range(2)] + [("in", m) for m in range(16, 20)]
          + [("sg", m) for m in range(4)] + [("in", m) for m in range(12, 16)]
          + [("out", m) for m in range(8)] + [("q", 0), "ssq1"] + [("q", m) for m in range(1, 8)]
          + [("s", t, h) for t in range(2) for h in range(2)] + ["sS"] + [("pT", h) for h in range(4)]
          + [("o", m) for m in range(4)] + ["pST"] + [("o", m) for m in range(4, 8)] + ["oS", "oST"] + [("xo", m) for m in range(8)]
          + ["lg", "ssq2", "lgT"] + [("htok", n) for n in range(6)] + ["rank", "gT"] + [("ga", n) for n in range(4)])
G = {name: n for n, name in enumerate(GROUPS)}
NG = len(GROUPS)
CONSTS = 11


def build(nc, x_t, mem_t, w_k, w_v, w_in, w_out, w_q, w_xo, kc, vc, w_gu, w_dn, params, ws_t,
          b_down, y_t, mk_t, mv, conv_p, conv_s, chunk_v):
    front_dram = {"w_k": w_k, "w_v": w_v, "w_in": w_in, "w_out": w_out, "w_q": w_q, "w_xo": w_xo,
                  "kc": kc, "vc": vc}
    with ExitStack() as ctx:
        def sb(name, shape, dt=F32):
            return ctx.enter_context(nc.sbuf_tensor(name, shape, dt))

        def sem(name):
            return ctx.enter_context(nc.semaphore(name))

        ring = sb("ring", [P, RING, SLOT])
        resid = sb("resid", [P, KT, T])
        par = sb("par", [P, NPARAM])
        ones = sb("ones", [P, P])
        ident = sb("ident", [P, P])
        before = sb("before", [P, P])
        blocks = sb("blocks", [P, P])
        slot_i = sb("slot_i", [P, SLOTS], I32)
        slot_no = sb("slot_no", [P, SLOTS])
        limit_i = sb("limit_i", [P, 4], I32)
        limits = sb("limits", [P, 4])
        sixty4 = sb("sixty4", [P, 4])
        valid = sb("valid", [P, TT])
        eps = sb("eps", [P, 1])
        warm = sb("warm", [P, 1])
        ssum = sb("ssum", [P, 3 * P])
        rstd_tok = sb("rstd_tok", [P, TT])
        rstd = sb("rstd", [P, 2, T])
        rank = sb("rank", [P, TT, NE])
        gate = sb("gate", [P, TT, NE])
        iters = sb("iters", [1, 1], I32)
        arena = sb("arena", [P, 20700])

        def view(at, *shape):
            n = int(np.prod(shape))
            v = arena[:, at:at + n]
            if len(shape) == 2:
                v = v.rearrange("p (a b) -> p a b", a=shape[0])
            elif len(shape) == 3:
                v = v.rearrange("p (a b c) -> p a b c", a=shape[0], b=shape[1])
            elif len(shape) == 4:
                v = v.rearrange("p (a b c d) -> p a b c d", a=shape[0], b=shape[1], c=shape[2])
            return v

        proj = view(0, 20, T)
        q_fm = view(0, KT, T)
        o_fm = view(8 * T, KT, T)
        small = view(16 * T, 4 * T)
        at = 20 * T
        v_tok = view(at, 2, 512)
        ws = view(at + 1024, 8, P)
        probs = view(at, 2, 4, NMEM)
        at += 2048
        zp = view(at, 4, NP_ + 2)
        at += 4 * (NP_ + 2)
        zs = view(at, 4, 3, NS)
        at += 96
        conv = view(at, 4, T)
        at += 4 * T
        mem = view(at, KT, NMEM)
        q_diag = view(at, KT, NS, 32)
        at += 2048
        k_fm = view(at, KT, NMEM)
        probs_t = view(at, 4, 2, NP_)
        at += 2048
        v_mem = view(at, 2, D)
        mem_raw = view(at, KT, NMEM)
        at += 2048
        sq = view(at, KT, T)
        p_diag = view(at, NS, 2, HEADS, 32)
        sq_at = at
        at += KT * T
        p_flat = view(sq_at, NS * 2 * HEADS * 32)
        s_s = view(at, NMEM)
        s_st = view(at + 256, 2, P)
        o_s = view(at + 512, NMEM)
        at += 768
        h_fm = view(at, KT, T)
        h_at = at
        at += KT * T
        assert at <= 20700, at
        lT = small[0:NE, 0:384]
        lg = small[:, 384:480].rearrange("p (a b) -> p a b", a=TT)
        gt4 = small[:, 480:608].rearrange("p (a b) -> p a b", a=TT + 1)
        gt = gt4[:, 0:TT, :]
        eq = small[:, 608:704].rearrange("p (a b) -> p a b", a=TT)
        cum = small[:, 704:800].rearrange("p (a b) -> p a b", a=TT)
        ex = small[:, 800:896].rearrange("p (a b) -> p a b", a=TT)
        top8 = small[:, 896:920].rearrange("p (a b) -> p a b", a=TT)
        cnt3 = small[:, 920:923]
        gsum = small[:, 923:926]
        cmax = small[:, 926:927]
        over = small[:, 927:931]
        nover = small[:, 931:932]
        att_m = small[:, 932:942]
        att_s = small[:, 942:952]
        at = 20 * T
        h_tok = view(at, TT, D)
        at += TT * D
        p_hot = view(at, TT, 4 * SLOTS)
        at += TT * 4 * SLOTS
        w_hot = view(at, TT, 4 * SLOTS)
        at += TT * 4 * SLOTS
        xg = view(at, 2, KT, 4 * SLOTS)
        at += 2 * KT * 4 * SLOTS
        gu_sb = view(at, D)
        assert at + D <= sq_at
        y_hot = view(0, 2, D)
        tb = view(2 * D, KT, 2 * SLOTS)
        sig = view(3 * D, KT, SLOTS)
        hid = view(3 * D + KT * SLOTS, KT, SLOTS)
        assert 4 * D <= 16 * T
        g_hot = view(sq_at, 2, T)
        gate_t = view(sq_at + 2 * T, T)
        bdn = view(sq_at + 3 * T, D)
        assert 3 * T + D <= KT * T

        ps = ctx.enter_context(nc.psum_tensor("ps", [P, 8, 512], F32))

        def bank(name):
            return ps[:, G[name] % 8, :]

        def par_of(name):
            a, b = PARAM_AT[name]
            return par[:, a:b]

        g_v, w00 = par_of("g_v"), par_of("w00")
        w_conv = par_of("w_conv").rearrange("p (k m) -> p k m", k=3)
        state = par_of("state").rearrange("p (m k s) -> p m k s", m=4, k=2)
        b_sp = par_of("b_sp").rearrange("p (m t) -> p m t", m=4)
        b_gu = par_of("b_gu").rearrange("p (e h m) -> p e h m", e=NE, h=2)
        router = par_of("router").rearrange("p (k e) -> p k e", k=KT)

        x_in, gains_in, par_in, ws_in, bdn_in = (
            sem(n) for n in ("x_in", "gains_in", "par_in", "ws_in", "bdn_in"))
        mem_in = [sem(f"mem_in{n}") for n in range(2)]
        landed = [sem(f"landed{n}") for n in range(RING)]
        half_landed = sem("half_landed")
        kv_stored = sem("kv_stored")
        mix_stored = sem("mix_stored")
        y_stored = sem("y_stored")
        grp = sem("grp")
        emptied = sem("emptied")
        kc_used = sem("kc_used")
        vc_used = sem("vc_used")
        const_ready = sem("const_ready")
        pool_step = sem("pool_step")
        dve_step = sem("dve_step")
        sq_ready = sem("sq_ready")
        sum_ready = sem("sum_ready")
        std_ready = sem("std_ready")
        rstd_ready = sem("rstd_ready")
        h_ready = sem("h_ready")
        mem_ready = sem("mem_ready")
        v_act = sem("v_act")
        v_sq = sem("v_sq")
        v_std = sem("v_std")
        v_norm = sem("v_norm")
        u_act = sem("u_act")
        ws_masked = sem("ws_masked")
        z_zero = sem("z_zero")
        z_ready = sem("z_ready")
        a_ready = sem("a_ready")
        b_ready = sem("b_ready")
        qd_zero = sem("qd_zero")
        qd_ready = sem("qd_ready")
        pd_zero = sem("pd_zero")
        pd_ready = sem("pd_ready")
        max_ready = sem("max_ready")
        s_exp = sem("s_exp")
        os_ready = sem("os_ready")
        lt_zero = sem("lt_zero")
        ex_in = sem("ex_in")
        ex_out = sem("ex_out")
        sel_ready = sem("sel_ready")
        gate_ready = sem("gate_ready")
        rank_ready = sem("rank_ready")
        iters_ready = sem("iters_ready")
        tok_copied = sem("tok_copied")
        gates_zero = sem("gates_zero")
        late_zero = sem("late_zero")
        p_built = sem("p_built")
        w_built = sem("w_built")
        rank_cut = sem("rank_cut")
        w_used = sem("w_used")
        gu_done = sem("gu_done")
        gu_copied = sem("gu_copied")
        t_done = sem("t_done")
        t_read = sem("t_read")
        g_ready = sem("g_ready")
        u_ready = sem("u_ready")
        ug_ready = sem("ug_ready")
        sig_ready = sem("sig_ready")
        hid_ready = sem("hid_ready")
        d_done = sem("d_done")
        y_copied = sem("y_copied")
        side_filled = sem("side_filled")
        side_copied = sem("side_copied")
        c_filled = sem("c_filled")
        c_added = sem("c_added")
        final_ssq = sem("final_ssq")
        y_done = sem("y_done")

        block = ctx.enter_context(nc.Block())

        def front_free(eng, n):
            kind, c = FRONT_CHUNKS[n]
            if kind == "kc" and c < NS - 1:
                eng.wait_ge(kc_used, c + 1)
            elif kind == "vc" and c < NS - 1:
                eng.wait_ge(vc_used, c + 1)
            else:
                last = {"w_k": ("k", 2 * c + 1), "w_v": ("v", c, 1), "w_in": ("in", 2 * c + 1),
                        "w_out": ("out", 2 * c + 1), "w_q": ("q", 2 * c + 1), "w_xo": ("xo", 2 * c + 1),
                        "kc": "sS", "vc": "oS"}[kind]
                eng.wait_ge(grp, G[last] + 1)

        def front_uses(slot):
            return len(range(slot, NF, RING))

        def slot_of(c):
            return (NF + c) % RING

        def columns(t, first):
            quads = t[:].rearrange("p a (q c) -> p a q c", c=4)
            return quads[:, :, bass.ds(first, 1), :].rearrange("p a q c -> p a (q c)")

        def hot(t):
            return t[:].rearrange("p a (e s) -> p a e s", e=4)

        @block.sync
        def _(sp):
            for half in range(2):
                sp.dma_start(mem_raw[:, 4 * half:4 * half + 4, :], mem_t[:, 4 * half:4 * half + 4, :]).then_inc(mem_in[half], 16)
                sp.dma_start(ring[:, 0, 1024 * half:1024 * half + 1024],
                             w_k[0, :, 1024 * half:1024 * half + 1024]).then_inc(landed[0] if half else half_landed, 16)
            for n, (kind, c) in enumerate(FRONT_CHUNKS):
                if n == 2:
                    sp.dma_start(resid[:], x_t).then_inc(x_in, 16)
                if n == 0:
                    continue
                if n >= RING:
                    front_free(sp, n - RING)
                sp.dma_start(ring[:, n % RING, :], front_dram[kind][c]).then_inc(landed[n % RING], 16)

            def expert_chunk(e, c):
                dst = ring[:, slot_of(c), :]
                if c < 8:
                    src = w_gu[bass.ds(e, 1), c].rearrange("a p n -> (a p) n")
                else:
                    dst = dst.rearrange("p (k n) -> p k n", k=2)
                    src = w_dn[bass.ds(e, 1), 2 * (c - 8):2 * (c - 8) + 2].rearrange("a k p n -> p (a k) n")
                sp.dma_start(dst, src).then_inc(landed[slot_of(c)], 16)

            for c in range(RING):
                front_free(sp, NF - RING + c)
                expert_chunk(0, c)

            def expert_loads(e, expert):
                for c in range(RING):
                    if c == 7:
                        sp.wait_ge(gu_done, e)
                    elif c == 11:
                        sp.wait_ge(d_done, e)
                    else:
                        sp.wait_ge(w_used, e * 10 - 9 + (c if c < 7 else c - 1))
                    expert_chunk(expert, c)

            with sp.Fori(1, NE) as e:
                expert_loads(e, e)
            sp.wait_ge(iters_ready, 1)
            end = sp.value_load(iters[0:1, 0:1], min_val=4, max_val=20)
            with sp.If(end > 4):
                with sp.Fori(1, end >> 2) as again:
                    with sp.Fori(0, NE) as expert:
                        expert_loads(again * NE + expert, expert)
            for m in range(0, KT, 2):
                sp.wait_ge(y_done, m + 2)
                sp.dma_start(y_t[:, m:m + 2, :], resid[:, m:m + 2, :]).then_inc(y_stored, 16)
            sp.wait_ge(y_stored, 16 * KT // 2)
            sp.wait_ge(kv_stored, 32)
            sp.wait_ge(mix_stored, 48)

        @block.gpsimd
        def _(pool):
            counts = {}
            pool.sem_inc(gates_zero, 1)

            def step(ins, s=pool_step):
                counts[s.name] = counts.get(s.name, 0) + 1
                ins.then_inc(s, 1)
                pool.wait_ge(s, counts[s.name])

            step(nc.gpsimd.memset(eps[:], EPS), const_ready)
            step(nc.gpsimd.memset(ssum[:, T:], 0.0), const_ready)
            step(nc.gpsimd.memset(ones[:], 1.0), const_ready)
            step(nc.gpsimd.memset(ident[:], 0.0))
            step(nc.gpsimd.memset(blocks[:], 0.0))
            step(nc.gpsimd.memset(valid[:], 1.0))
            step(nc.gpsimd.affine_select(out=ident[:], in_=ident[:], compare_op=ALU.not_equal, fill=1.0, base=0,
                                    pattern=[[-1, P]], channel_multiplier=1), const_ready)
            step(nc.gpsimd.affine_select(out=before[:], in_=ones[:], compare_op=ALU.is_gt, fill=0.0, base=0,
                                    pattern=[[1, P]], channel_multiplier=-1), const_ready)
            step(nc.gpsimd.memset(blocks[0:64, 0:64], 1.0), const_ready)
            step(nc.gpsimd.memset(blocks[64:128, 64:128], 1.0), const_ready)
            step(nc.gpsimd.affine_select(out=valid[:, 2:3], in_=valid[:, 2:3], compare_op=ALU.is_ge, fill=0.0, base=NS - 1,
                                    pattern=[[0, 1]], channel_multiplier=-1), const_ready)
            step(nc.gpsimd.iota(slot_i[:], pattern=[[1, SLOTS]], base=0, channel_multiplier=0))
            step(nc.gpsimd.iota(limit_i[:], pattern=[[SLOTS, 4]], base=SLOTS, channel_multiplier=0))
            step(nc.gpsimd.tensor_copy(slot_no[:], slot_i[:]), const_ready)
            step(nc.gpsimd.tensor_copy(limits[:], limit_i[:]), const_ready)
            step(nc.gpsimd.memset(sixty4[:], float(SLOTS)), const_ready)
            step(nc.gpsimd.memset(zp[:, :, 0:2], 0.0), z_zero)
            pool.wait_ge(ws_in, 16)
            step(nc.gpsimd.affine_select(out=ws[:], in_=ws[:], compare_op=ALU.is_ge, fill=0.0, base=0,
                                    pattern=[[0, 8], [1, P]], channel_multiplier=-1), ws_masked)
            pool.wait_ge(grp, G[("v", 3, 1)] + 1)
            step(nc.gpsimd.memset(q_diag[:], 0.0), qd_zero)
            pool.wait_ge(sum_ready, 3)
            step(nc.gpsimd.memset(p_diag[:], 0.0), pd_zero)
            pool.wait_ge(grp, G[("out", 7)] + 1)
            step(nc.gpsimd.memset(lT, 0.0), lt_zero)
            step(nc.gpsimd.memset(gt4[:, TT, :], 0.0), lt_zero)
            pool.wait_ge(grp, G[("pT", 3)] + 1)
            pool.wait_ge(grp, G["oS"] + 1)
            pool.wait_ge(mix_stored, 48)
            step(nc.gpsimd.memset(h_tok[:, 2, :], 0.0), late_zero)
            pool.wait_ge(sum_ready, 4)
            step(nc.gpsimd.memset(gate_t[:], 0.0), late_zero)
            step(nc.gpsimd.memset(bdn[:], 0.0), late_zero)
            step(nc.gpsimd.memset(g_hot[:, 1, :], 0.0), late_zero)
            pool.wait_ge(grp, G[("xo", 7)] + 1)
            step(nc.gpsimd.memset(y_hot[:, 1, :], 0.0), late_zero)
            def build_w(first, number):
                nc.gpsimd.tensor_tensor(hot(w_hot), hot(p_hot), columns(gate, first).unsqueeze(3).to_broadcast([P, TT, 4, SLOTS]),
                                        ALU.mult).then_inc(w_built, 1)
                pool.wait_ge(w_built, number)
                nc.gpsimd.tensor_tensor(columns(rank, first), columns(rank, first),
                                        sixty4[:].unsqueeze(1).to_broadcast([P, TT, 4]), ALU.subtract).then_inc(rank_cut, 1)
                pool.wait_ge(rank_cut, number)

            pool.wait_ge(rank_ready, 1)
            pool.wait_ge(gate_ready, 1)
            pool.wait_ge(p_built, 1)
            build_w(0, 1)
            pool.wait_ge(grp, G[("ga", 3)] + 1)
            pool.wait_ge(iters_ready, 1)
            end = pool.value_load(iters[0:1, 0:1], min_val=4, max_val=20)
            with pool.Fori(0, end) as it:
                for half in range(2):
                    quad = it * 2 + half
                    first = (quad + 1) & 7
                    pool.wait_ge(side_filled, quad * 6 + 4 + 1)
                    pool.wait_ge(p_built, quad + 2)
                    build_w(first, quad + 2)
                pool.wait_ge(c_filled, it * 32 + 24)
                nc.gpsimd.tensor_tensor(gate_t[:], gate_t[:], gate_t[:], ALU.subtract).then_inc(gates_zero, 1)

        @block.scalar
        def _(act):
            for credit in (gu_copied, y_copied, side_copied):
                act.sem_inc(credit, 1)
            act.dma_start(par[:, 0:NGAIN], params[:, 0:NGAIN]).then_inc(gains_in, 16)

            def emptied_by(name):
                act.wait_ge(emptied, G[name] + 1)

            def root(name, v, mean_of=D):
                act.wait_ge(grp, G[name] + 1)
                ins = nc.scalar.activation(v, bank(name)[:, 0:v.shape[-1]], ACT.Sqrt, bias=eps[:], scale=1.0 / mean_of)
                ins.then_inc(std_ready, 1)

            for half in range(2):
                act.wait_ge(mem_in[half], 16)
                nc.scalar.activation(sq[:, 4 * half:4 * half + 4, 0:NMEM], mem_raw[:, 4 * half:4 * half + 4, :],
                                     ACT.Square).then_inc(sq_ready, 1)
            act.wait_ge(const_ready, CONSTS)
            root("mem_ssq", rstd[:, 0, 0:NMEM + 2])
            act.wait_ge(x_in, 16)
            act.wait_ge(sum_ready, 1)
            nc.scalar.activation(sq[:], resid[:], ACT.Square).then_inc(sq_ready, 1)
            act.dma_start(par[:, NGAIN:], params[:, NGAIN:]).then_inc(par_in, 16)
            act.dma_start(ws[:], ws_t).then_inc(ws_in, 16)
            root("ssq0", rstd[:, 1, :])
            emptied_by(("k", 7))
            act.dma_start(mk_t, k_fm[:]).then_inc(kv_stored, 16)
            emptied_by(("v", 3, 1))
            act.dma_start(mv, v_mem[:]).then_inc(kv_stored, 16)
            for m in range(4):
                emptied_by(("in", 4 + m))
                nc.scalar.activation(proj[:, 4 + m, :], proj[:, 4 + m, :], ACT.Gelu).then_inc(v_act, 1)
            for m in range(4):
                act.wait_ge(v_act, m + 1)
                nc.scalar.activation(sq[:, m, :], proj[:, 4 + m, :], ACT.Square).then_inc(v_sq, 1)
            for m in range(4):
                emptied_by(("in", m))
                nc.scalar.activation(proj[:, m, :], proj[:, m, :], ACT.Gelu).then_inc(u_act, 1)
            for m in range(4):
                act.wait_ge(grp, G[("vssq", m)] + 1)
                nc.scalar.activation(sq[:, 4 + m, :], bank(("vssq", m))[:, 0:T], ACT.Sqrt, bias=eps[:],
                                     scale=1.0 / 64).then_inc(v_std, 1)
            act.wait_ge(v_norm, 4)
            act.dma_start(chunk_v, proj[:, 4:8, NP_:T]).then_inc(mix_stored, 16)
            act.wait_ge(z_ready, 2)
            act.dma_start(conv_p, zp[:, :, NP_:NP_ + 2]).then_inc(mix_stored, 16)
            act.dma_start(conv_s, zs[:, :, 1:3, :]).then_inc(mix_stored, 16)
            for m in range(KT):
                emptied_by(("out", m))
                nc.scalar.activation(sq[:, m, :], resid[:, m, :], ACT.Square).then_inc(sq_ready, 1)
            root("ssq1", rstd[:, 0, :])
            nc.scalar.activation(warm[:], eps[:], ACT.Exp)
            for n in range(4):
                act.wait_ge(max_ready, n + 1)
                for hh in range(2):
                    h = 2 * (n % 2) + hh
                    ins = nc.scalar.activation(probs[:, n // 2, h, :], bank(("s", n // 2, n % 2))[:, NMEM * hh:NMEM * hh + NMEM],
                                               ACT.Exp, bias=att_m[:, 2 * n + hh:2 * n + hh + 1], scale=1.0 / 16.0,
                                               accum_out=att_s[:, 2 * n + hh:2 * n + hh + 1])
                ins.then_inc(s_exp, 1)
            act.wait_ge(max_ready, 5)
            nc.scalar.activation(s_s[:], bank("sS")[:, 0:NMEM], ACT.Exp, bias=att_m[:, 8:9], scale=1.0 / 16.0,
                                 accum_out=att_s[:, 8:9]).then_inc(s_exp, 1)
            act.wait_ge(grp, G["oS"] + 1)
            for m in range(KT):
                emptied_by(("xo", m))
                nc.scalar.activation(sq[:, m, :], resid[:, m, :], ACT.Square).then_inc(sq_ready, 1)
            root("ssq2", rstd_tok[:])
            nc.scalar.activation(warm[:], eps[:], ACT.Exp)
            act.wait_ge(late_zero, 1)
            act.wait_ge(rstd_ready, 4)
            for n in range(6):
                rows = P if n < 4 else NS
                if n == 3:
                    act.wait_ge(ex_in, 1)
                    nc.scalar.activation(ex[:], ex[:], ACT.Exp).then_inc(ex_out, 1)
                act.wait_ge(grp, G[("htok", n)] + 1)
                nc.scalar.activation(h_tok[0:rows, n // 2, 512 * (n % 2):512 * (n % 2) + 512], bank(("htok", n))[0:rows],
                                     ACT.Copy, scale=rstd_tok[0:rows, n // 2:n // 2 + 1]).then_inc(tok_copied, 1)
            act.wait_ge(late_zero, 5)
            act.dma_start(bdn[0:NE, :], b_down).then_inc(bdn_in, 16)

            act.wait_ge(iters_ready, 1)
            end = act.value_load(iters[0:1, 0:1], min_val=4, max_val=20)
            act.wait_ge(emptied, NG)
            with act.Fori(0, end) as it:
                for j in range(8):
                    e, i, quad, nxt = it * 8 + j, j % 4, it * 2 + j // 4, (j // 4 + 1) % 2
                    act.wait_ge(gu_done, e + 1)
                    act.wait_ge(t_done, e + 1)
                    nc.scalar.activation(gu_sb.rearrange("p (a b) -> p a b", a=2), ps[:, 0:2, :],
                                         ACT.Copy).then_inc(gu_copied, 1)
                    pos = quad * 6 + (0, 2, 3, 5)[i]
                    if i % 2 == 0:
                        act.wait_ge(side_filled, pos + 2)
                        nc.scalar.activation(g_hot[:, i // 2, :], ps[:, 5, 0:T], ACT.Copy).then_inc(side_copied, 1)
                        pos = pos + 1
                    act.wait_ge(g_ready, e + 1)
                    nc.scalar.activation(sig[:], tb[:, :, 0:SLOTS], ACT.Sigmoid, scale=ALPHA).then_inc(sig_ready, 1)
                    act.wait_ge(side_filled, pos + 2)
                    nc.scalar.activation(xg[:, nxt, 2 * i:2 * i + 2, :], ps[:, 5, :].rearrange("p (a b) -> p a b", a=2),
                                         ACT.Copy).then_inc(side_copied, 1)
                    act.wait_ge(d_done, e + 1)
                    row = SLOTS * (i % 2)
                    nc.scalar.activation(y_hot[row:row + 64, i // 2, 0:512], ps[0:64, 4, :], ACT.Copy)
                    nc.scalar.activation(y_hot[row:row + 64, i // 2, 512:1024], ps[64:128, 4, :],
                                         ACT.Copy).then_inc(y_copied, 1)
            for m in range(KT):
                act.wait_ge(c_added, end * 32 + m + 2)
                nc.scalar.activation(h_fm[:, m, :], resid[:, m, :], ACT.Square).then_inc(sq_ready, 1)
            act.wait_ge(final_ssq, 1)
            nc.scalar.activation(rstd[:, 0, :], ps[:, 0, 0:T], ACT.Sqrt, bias=eps[:], scale=1.0 / D).then_inc(std_ready, 1)

        @block.vector
        def _(dve):
            for credit in (t_read, c_added):
                dve.sem_inc(credit, 1)
            TTN, TS, STT = nc.vector.tensor_tensor, nc.vector.tensor_scalar, nc.vector.scalar_tensor_tensor
            copy = nc.vector.tensor_copy
            steps = [0]

            def link(ins):
                steps[0] += 1
                ins.then_inc(dve_step, 1)
                dve.wait_ge(dve_step, steps[0])

            def filled(name, width=512):
                dve.wait_ge(grp, G[name] + 1)
                return bank(name)[:, 0:width]

            def bc(v, axis, shape):
                return v.unsqueeze(axis).to_broadcast(shape)

            def add_squares(src, m, first_square):
                if m == 0:
                    return
                dve.wait_ge(sq_ready, first_square + m)
                a = src[:, 0, :] if m == 1 else ssum[:, 0:T]
                ins = TTN(ssum[:, 0:T], a, src[:, m, :], ALU.add)
                if m < KT - 1:
                    link(ins)
                else:
                    ins.then_inc(sum_ready, 1)

            def inverse(n, v):
                dve.wait_ge(std_ready, n)
                nc.vector.reciprocal(v, v).then_inc(rstd_ready, 1)
                dve.wait_ge(rstd_ready, n)

            def build_p(quad):
                slots = slot_no[:].unsqueeze(1).unsqueeze(1).to_broadcast([P, TT, 4, SLOTS])
                ranks = columns(rank, quad).unsqueeze(3).to_broadcast([P, TT, 4, SLOTS])
                TTN(hot(p_hot), slots, ranks, ALU.is_equal).then_inc(p_built, 1)

            dve.wait_ge(gains_in, 16)
            for k in range(KT):
                dve.wait_ge(mem_in[k // 4], 16)
                TS(mem[:, k, :], mem_raw[:, k, :], par_of("g_mem")[:, k:k + 1], None, ALU.mult).then_inc(mem_ready, 1)
            dve.wait_ge(sq_ready, 2)
            nc.vector.tensor_reduce(ssum[:, 0:NMEM], sq[:, :, 0:NMEM].rearrange("p k t -> p t k"), AX.X,
                                    ALU.add).then_inc(sum_ready, 1)
            dve.wait_ge(x_in, 16)
            for k in range(KT):
                TS(h_fm[:, k, :], resid[:, k, :], par_of("g_mix")[:, k:k + 1], None, ALU.mult).then_inc(h_ready, 1)
            inverse(1, rstd[:, 0, 0:NMEM + 2])

            def mem_key(m):
                TTN(k_fm[:, m, :], filled(("k", m), NMEM), rstd[:, 0, 0:NMEM], ALU.mult).then_inc(emptied, 2 if m == 2 else 1)

            for m in range(5):
                mem_key(m)
            dve.wait_ge(sq_ready, 3)
            nc.vector.tensor_reduce(ssum[:, 0:T], sq.rearrange("p k t -> p t k"), AX.X, ALU.add).then_inc(sum_ready, 1)
            for m in range(5, KT):
                mem_key(m)
            for c in range(4):
                for t in range(2):
                    if (c, t) == (1, 0):
                        inverse(2, rstd[:, 1, :])
                    TS(v_mem[:, t, 256 * c:256 * c + 256], filled(("v", c, t), 256), rstd[:, 0, NMEM + t:NMEM + t + 1],
                       None, ALU.mult).then_inc(emptied, 2 if (c, t) == (1, 0) else 1)
            dve.wait_ge(par_in, 16)

            def projected(m, n=1):
                TTN(proj[:, m, :], filled(("in", m), T), rstd[:, n, :], ALU.mult).then_inc(emptied, 1)

            for m in range(4, 8):
                projected(m)
            for m in range(4):
                projected(m)
            for m in range(4):
                dve.wait_ge(v_std, m + 1)
                nc.vector.reciprocal(sq[:, 4 + m, :], sq[:, 4 + m, :]).then_inc(emptied, 1)
                dve.wait_ge(emptied, G[("vssq", m)] + 1)
                STT(proj[:, 4 + m, :], proj[:, 4 + m, :], g_v[:, m:m + 1], sq[:, 4 + m, :],
                    ALU.mult, ALU.mult).then_inc(v_norm, 1)
            for m in range(8, 12):
                projected(m)
            for c in range(2):
                copy(v_tok[:, c, :], filled(("vtok", c))).then_inc(emptied, 1)
            for m in range(16, 20):
                projected(m)
            dve.wait_ge(emptied, G[("in", 19)] + 1)
            TTN(zp[:, :, 2:], proj[:, 16:20, 0:NP_], proj[:, 8:12, 0:NP_], ALU.mult).then_inc(z_ready, 1)
            copy(zs[:, :, 0:2, :], state).then_inc(dve_step, 1)
            steps[0] += 1
            TTN(zs[:, :, 2, :], proj[:, 16:20, NP_:T], proj[:, 8:12, NP_:T], ALU.mult).then_inc(z_ready, 1)
            dve.wait_ge(z_ready, 2)
            dve.wait_ge(z_zero, 1)
            dve.wait_ge(u_act, 4)
            dve.wait_ge(v_norm, 4)
            for m in range(4):
                gated = conv[:, m, 0:NP_].rearrange("p (c t) -> p c t", c=2)
                TTN(gated, filled(("sg", m), NP_).rearrange("p (c t) -> p c t", c=2),
                    bc(b_sp[:, m, :], 1, [P, 2, P]), ALU.add).then_inc(emptied, 1)
                link(TS(conv[:, m, NP_:T], proj[:, 4 + m, NP_:T], w00[:, m:m + 1], b_sp[:, m, 0:1], ALU.mult, ALU.add))
                dve.wait_ge(emptied, G[("sg", m)] + 1)
                TTN(proj[:, m, :], proj[:, m, :], conv[:, m, :], ALU.mult).then_inc(a_ready, 1)
            dve.wait_ge(a_ready, 4)
            for m in range(4):
                TS(conv[:, m, 0:NP_], zp[:, m, 0:NP_], w_conv[:, 0, m:m + 1], None, ALU.mult)
                link(TS(conv[:, m, NP_:T], zs[:, m, 0, :], w_conv[:, 0, m:m + 1], None, ALU.mult))
            for k in range(1, 3):
                for m in range(4):
                    STT(conv[:, m, 0:NP_], zp[:, m, k:k + NP_], w_conv[:, k, m:m + 1], conv[:, m, 0:NP_], ALU.mult, ALU.add)
                    ins = STT(conv[:, m, NP_:T], zs[:, m, k, :], w_conv[:, k, m:m + 1], conv[:, m, NP_:T], ALU.mult, ALU.add)
                    ins.then_inc(dve_step, 1)
                    steps[0] += 1
                dve.wait_ge(dve_step, steps[0])
            for m in range(4):
                projected(12 + m)
                dve.wait_ge(emptied, G[("in", 12 + m)] + 1)
                TTN(proj[:, 12 + m, :], proj[:, 12 + m, :], conv[:, m, :], ALU.mult).then_inc(b_ready, 1)
            for m in range(KT):
                TTN(resid[:, m, :], resid[:, m, :], filled(("out", m), T), ALU.add).then_inc(emptied, 1)
                dve.wait_ge(emptied, G[("out", m)] + 1)
                TS(h_fm[:, m, :], resid[:, m, :], par_of("g_xattn")[:, m:m + 1], None, ALU.mult).then_inc(h_ready, 1)
                if m:
                    add_squares(sq, m - 1, 4)
            add_squares(sq, KT - 1, 4)
            inverse(3, rstd[:, 0, :])
            dve.wait_ge(mix_stored, 48)
            for m in range(KT):
                TTN(q_fm[:, m, :], filled(("q", m), T), rstd[:, 0, :], ALU.mult).then_inc(emptied, 2 if m == 1 else 1)
            dve.wait_ge(qd_zero, 1)
            dve.wait_ge(emptied, G[("q", 7)] + 1)
            diag = q_diag.rearrange("p k s c -> p k (s c)")[:, :, 0:(NS - 1) * 33 + 1:33]
            copy(diag, q_fm[:, :, NP_:T]).then_inc(qd_ready, 1)
            def normalise(n):
                dve.wait_ge(s_exp, n + 1)
                link(nc.vector.reciprocal(att_s[:, 2 * n:2 * n + 2], att_s[:, 2 * n:2 * n + 2]))
                for hh in range(2):
                    v = probs[:, n // 2, 2 * (n % 2) + hh, :]
                    TS(v, v, att_s[:, 2 * n + hh:2 * n + hh + 1], None, ALU.mult).then_inc(
                        emptied if hh else dve_step, 1)
                steps[0] += 1

            for n in range(4):
                b = filled(("s", n // 2, n % 2)).rearrange("p (h c) -> p h c", h=2)
                top = att_m[:, 2 * n:2 * n + 2]
                link(nc.vector.tensor_reduce(top, b, AX.X, ALU.max))
                TS(top, top, -1.0 / 16.0, None, ALU.mult).then_inc(max_ready, 1)
            for n in range(2):
                normalise(n)
            link(nc.vector.tensor_reduce(att_m[:, 8:9], filled("sS", NMEM), AX.X, ALU.max))
            TS(att_m[:, 8:9], att_m[:, 8:9], -1.0 / 16.0, None, ALU.mult).then_inc(max_ready, 1)
            for n in range(2, 4):
                normalise(n)
            dve.wait_ge(s_exp, 5)
            link(nc.vector.reciprocal(att_s[:, 8:9], att_s[:, 8:9]))
            TS(s_s[:], s_s[:], att_s[:, 8:9], None, ALU.mult).then_inc(emptied, 1)
            dve.wait_ge(kv_stored, 32)
            for h in range(HEADS):
                copy(probs_t[:, h, :, :], filled(("pT", h)).rearrange("p (m q) -> p m q", m=2)).then_inc(emptied, 1)
            for m in range(KT):
                if m == 4:
                    copy(s_st[:], filled("pST", 256).rearrange("p (m r) -> p m r", m=2)).then_inc(emptied, 1)
                    dve.wait_ge(pd_zero, 1)
                    dve.wait_ge(emptied, G["pST"] + 1)
                    for mt in range(2):
                        for h in range(HEADS):
                            flat = p_flat[:, (mt * HEADS + h) * 32:(mt * HEADS + h) * 32 + (NS - 1) * 257 + 1:257]
                            copy(flat, s_st[:, mt, 32 * h:32 * h + NS]).then_inc(pd_ready, 1)
                copy(o_fm[:, m, 0:NP_], filled(("o", m), NP_)).then_inc(emptied, 1)
            copy(o_s[:], filled("oS", NMEM)).then_inc(emptied, 1)
            b = filled("oST", 256).rearrange("p (k h c) -> p h k c", k=2, h=HEADS)
            o_heads = o_fm.rearrange("p (h k) t -> p h k t", h=HEADS)
            for k in range(2):
                ins = copy(o_heads[:, :, k, NP_:T], b[:, :, k, 0:NS])
                ins.then_inc(os_ready if k == 0 else emptied, 1)
            for m in range(KT):
                TTN(resid[:, m, :], resid[:, m, :], filled(("xo", m), T), ALU.add).then_inc(emptied, 1)
                dve.wait_ge(emptied, G[("xo", m)] + 1)
                TS(h_fm[:, m, :], resid[:, m, :], par_of("g_moe")[:, m:m + 1], None, ALU.mult).then_inc(h_ready, 1)
                if m:
                    add_squares(sq, m - 1, 12)
            add_squares(sq, KT - 1, 12)
            dve.wait_ge(lt_zero, 2)
            copy(lT[:, 0:T], filled("lg", T)[0:NE]).then_inc(emptied, 1)
            inverse(4, rstd_tok[:])
            for t in range(TT):
                b = filled("lgT", 96)[:, NE * t:NE * t + NE]
                ins = STT(lg[:, t, :], b, rstd_tok[:, t:t + 1], par_of("b_router"), ALU.mult, ALU.add)
                if t < TT - 1:
                    ins.then_inc(dve_step, 1)
                    steps[0] += 1
                else:
                    ins.then_inc(emptied, 2)
            dve.wait_ge(dve_step, steps[0])
            dve.wait_ge(emptied, G["lgT"] + 1)
            for t in range(TT):
                ins = nc.vector.max(top8[:, t, :], lg[:, t, :])
                ins.then_inc(dve_step, 1)
            steps[0] += TT
            dve.wait_ge(dve_step, steps[0])
            TTN(ex[:], lg[:], top8[:, :, 0:1].to_broadcast([P, TT, NE]), ALU.subtract).then_inc(ex_in, 1)
            fourth = top8[:, :, TOPK - 1:TOPK].to_broadcast([P, TT, NE])
            link(TTN(gt[:], lg[:], fourth, ALU.is_gt))
            link(TTN(eq[:], lg[:], fourth, ALU.is_equal))
            link(nc.vector.tensor_reduce(cnt3, gt[:], AX.X, ALU.add))
            link(TS(cnt3, cnt3, -1.0, float(TOPK), ALU.mult, ALU.add))
            for t in range(TT):
                ins = (nc.vector.tensor_tensor_scan(cum[:, t, :], ones[:, 0:NE], eq[:, t, :], 0.0, ALU.mult, ALU.add))
                ins.then_inc(dve_step, 1)
            steps[0] += TT
            dve.wait_ge(dve_step, steps[0])
            link(TTN(cum[:], cum[:], bc(cnt3, 2, [P, TT, NE]), ALU.is_le))
            link(TTN(eq[:], eq[:], cum[:], ALU.mult))
            link(TTN(gt[:], gt[:], eq[:], ALU.add))
            TTN(gt[:], gt[:], bc(valid[:], 2, [P, TT, NE]), ALU.mult).then_inc(sel_ready, 1)
            dve.wait_ge(sel_ready, 1)
            dve.wait_ge(ex_out, 1)
            link(TTN(ex[:], ex[:], gt[:], ALU.mult))
            link(nc.vector.tensor_reduce(gsum, ex[:], AX.X, ALU.add))
            link(TS(gsum, gsum, 0.5, None, ALU.max))
            link(nc.vector.reciprocal(gsum, gsum))
            TTN(gate[:], ex[:], bc(gsum, 2, [P, TT, NE]), ALU.mult).then_inc(gate_ready, 1)
            dve.wait_ge(sel_ready, 1)
            b = filled("rank", 128)
            link(STT(rank[:], b[:, 0:96].rearrange("p (a e) -> p a e", a=TT), 1.0, gt[:], ALU.add, ALU.mult))
            TS(rank[:], rank[:], -1.0, None, ALU.add).then_inc(rank_ready, 1)
            dve.wait_ge(rank_ready, 1)
            build_p(0)
            nc.vector.tensor_reduce(cmax, b[:, 96:128], AX.X, ALU.max).then_inc(emptied, 7)
            dve.wait_ge(emptied, G["rank"] + 1)
            link(TTN(over, limits[:], cmax.to_broadcast([P, 4]), ALU.is_lt))
            link(nc.vector.tensor_reduce(nover, over, AX.X, ALU.add))
            TS(iters[:], nover[0:1, :], 4.0, 4.0, ALU.mult, ALU.add).then_inc(iters_ready, 1)
            dve.wait_ge(late_zero, 5)
            copy(gate_t[0:NE, :], filled("gT", T)[0:NE]).then_inc(emptied, 1)
            for n in range(4):
                copy(xg[:, 0, 2 * n:2 * n + 2, :], filled(("ga", n)).rearrange("p (a b) -> p a b", a=2)).then_inc(emptied, 1)
            dve.wait_ge(emptied, NG)

            def combine(n, m):
                dve.wait_ge(c_filled, n + 1)
                TTN(resid[:, m, :], resid[:, m, :], ps[:, 6 + m % 2, 0:T], ALU.add).then_inc(c_added, 1)

            dve.wait_ge(iters_ready, 1)
            end = dve.value_load(iters[0:1, 0:1], min_val=4, max_val=20)
            with dve.Fori(0, end) as it:
                expert0 = (it & 3) * 8
                for j in range(8):
                    e, i, quad = it * 8 + j, j % 4, it * 2 + j // 4
                    if i == 0:
                        dve.wait_ge(side_filled, quad * 6 + 1)
                        dve.wait_ge(rank_cut, quad + 1)
                        build_p((quad + 1) & 7)
                    dve.wait_ge(c_added, e * 4 + 1)
                    for r in range(2):
                        combine(e * 4 + r, 4 * (i % 2) + r)
                    dve.wait_ge(t_done, e + 2)
                    turned = ps[:, 2:4, :].rearrange("p a (k h s) -> p (a k) h s", h=2, s=SLOTS)
                    both = tb.rearrange("p k (h s) -> p k h s", h=2)
                    gate_v, up_v = tb[:, :, 0:SLOTS], tb[:, :, SLOTS:2 * SLOTS]
                    for h in range(2):
                        bias = b_gu[:, bass.ds(expert0 + j, 1), h, :].rearrange("p a m -> p (a m)")
                        TTN(both[:, :, h, :], turned[:, :, h, :], bc(bias, 2, [P, KT, SLOTS]),
                            ALU.add).then_inc(t_read, 1)
                        dve.wait_ge(t_read, e * 2 + 2 + h)
                        if h == 0:
                            TS(gate_v, gate_v, LIMIT, None, ALU.min).then_inc(g_ready, 1)
                        else:
                            TS(up_v, up_v, LIMIT, -LIMIT, ALU.min, ALU.max).then_inc(u_ready, 1)
                    dve.wait_ge(u_ready, e + 1)
                    dve.wait_ge(g_ready, e + 1)
                    STT(up_v, up_v, 1.0, gate_v, ALU.add, ALU.mult).then_inc(ug_ready, 1)
                    dve.wait_ge(sig_ready, e + 1)
                    dve.wait_ge(ug_ready, e + 1)
                    TTN(hid[:], up_v, sig[:], ALU.mult).then_inc(hid_ready, 1)
                    for r in range(2, 4):
                        combine(e * 4 + r, 4 * (i % 2) + r)
            dve.wait_ge(c_added, end * 32 + 1)
            for m in range(KT):
                dve.wait_ge(c_filled, end * 32 + m + 1)
                TTN(resid[:, m, :], resid[:, m, :], ps[:, (0, 1, 2, 3, 5, 6, 7, 4)[m], 0:T], ALU.add).then_inc(c_added, 1)
                if m:
                    add_squares(h_fm, m - 1, 20)
            add_squares(h_fm, KT - 1, 20)
            inverse(5, rstd[:, 0, :])
            dve.wait_ge(c_added, end * 32 + 8 + 1)
            for m in range(KT):
                STT(resid[:, m, :], resid[:, m, :], par_of("g_final")[:, m:m + 1], rstd[:, 0, :],
                    ALU.mult, ALU.mult).then_inc(y_done, 1)

        @block.tensor
        def _(pe):
            for credit in (t_done, side_filled):
                pe.sem_inc(credit, 1)
            mm, turn = nc.tensor.matmul, nc.tensor.transpose

            def begin(name):
                if G[name] >= 8:
                    before_it = GROUPS[G[name] - 8]
                    if before_it[0] == "htok":
                        pe.wait_ge(tok_copied, before_it[1] + 1)
                    else:
                        pe.wait_ge(emptied, G[name] - 7)
                return bank(name)

            def chunk(key):
                n = CHUNK_AT[key]
                pe.wait_ge(landed[n % RING], 16 * (n // RING + 1))
                return ring[:, n % RING, :]

            def sum_squares(name, n, width, token_tiles=0):
                b = begin(name)
                pe.wait_ge(sum_ready, n)
                if width:
                    last = mm(b[:, 0:width], ones[:], ssum[:, 0:width], start=True, stop=True)
                for t in range(token_tiles):
                    last = mm(b[:, width + t:width + t + 1], ssum[:, P * t:P * t + P], ones[:, 0:1], start=True, stop=True)
                last.then_inc(grp, 1)

            def project(kind, m, source, c=None, ready=None):
                first = (kind, m) == ("w_k", 0)
                w = (ring[:, 0, :] if first else chunk((kind, m // 2))).rearrange("p (k n) -> p k n", k=KT)
                b = begin((kind if c is None else c, m))
                src = source(0)
                width = src.shape[-1]
                for k in range(KT):
                    if first and k % 4 == 0:
                        pe.wait_ge(half_landed if k == 0 else landed[0], 16)
                    if ready is not None:
                        pe.wait_ge(ready[0], ready[1] + k + 1)
                    last = mm(b[:, 0:width], w[:, k, P * (m % 2):P * (m % 2) + P], source(k),
                              start=(k == 0), stop=(k == KT - 1))
                last.then_inc(grp, 1)

            pe.wait_ge(const_ready, 3)
            for _ in range(12):
                mm(ps[:, 7, 0:P], ones[:], ones[:], start=True, stop=True)
            for m in range(KT):
                project("w_k", m, lambda k: mem[:, k, :], "k", (mem_ready, 0) if m == 0 else None)
                if m == 1:
                    pe.wait_ge(const_ready, CONSTS)
                    sum_squares("mem_ssq", 1, NMEM, 2)
            for c in range(4):
                w = chunk(("w_v", c)).rearrange("p (k n) -> p k n", k=KT)
                for t in range(2):
                    b = begin(("v", c, t))
                    for k in range(KT):
                        last = mm(b[:, 0:256], mem[:, k, P * t:P * t + P], w[:, k, :], start=(k == 0), stop=(k == KT - 1))
                    last.then_inc(grp, 1)
                if c == 0:
                    sum_squares("ssq0", 2, T)
            pe.wait_ge(h_ready, KT)

            def gained(k):
                return h_fm[:, k, :]

            for m in (4, 5, 6, 7, 0, 1, 2, 3):
                project("w_in", m, gained, "in")
            for m in range(4):
                b = begin(("vssq", m))
                pe.wait_ge(v_sq, m + 1)
                mm(b[:, 0:T], blocks[:], sq[:, m, :], start=True, stop=True).then_inc(grp, 1)
            for m in range(8, 12):
                project("w_in", m, gained, "in")
            for c in range(2):
                b = begin(("vtok", c))
                for m in range(4):
                    pe.wait_ge(v_norm, m + 1)
                    last = turn(b[:, P * m:P * m + P], proj[:, 4 + m, P * c:P * c + P], ident[:])
                last.then_inc(grp, 1)
            for m in range(16, 20):
                project("w_in", m, gained, "in")
            pe.wait_ge(ws_masked, 1)
            pe.wait_ge(emptied, G[("vtok", 1)] + 1)
            for m in range(4):
                b = begin(("sg", m))
                for c in range(2):
                    for hh in range(2):
                        head = 2 * m + hh
                        last = mm(b[64 * hh:64 * hh + 64, P * c:P * c + P], v_tok[:, c, 64 * head:64 * head + 64],
                                  ws[:, head, :], start=True, stop=True)
                last.then_inc(grp, 1)
            for m in range(12, 16):
                project("w_in", m, gained, "in")

            def mixed(k):
                return proj[:, k if k < 4 else 8 + k, :]

            pe.wait_ge(a_ready, 4)
            pe.wait_ge(b_ready, 4)
            for m in range(KT):
                project("w_out", m, mixed, "out")
            for m in range(KT):
                project("w_q", m, gained, "q", (h_ready, KT) if m == 0 else None)
                if m == 0:
                    sum_squares("ssq1", 3, T)
            pe.wait_ge(emptied, G[("q", 7)] + 1)
            for t in range(2):
                for pair in range(2):
                    b = begin(("s", t, pair))
                    for hh in range(2):
                        for dk in range(2):
                            ft = 2 * (2 * pair + hh) + dk
                            last = mm(b[:, NMEM * hh:NMEM * hh + NMEM], q_fm[:, ft, P * t:P * t + P], k_fm[:, ft, :],
                                      start=(dk == 0), stop=(dk == 1))
                    last.then_inc(grp, 1)
            b = begin("sS")
            pe.wait_ge(qd_ready, 1)
            for t in range(NS):
                keys = chunk(("kc", t)).rearrange("p (k n) -> p k n", k=KT)
                for dk in range(2):
                    for h in range(HEADS):
                        last = mm(b[32 * h:32 * h + 32, 0:NMEM], q_diag[:, 2 * h + dk, t, :], keys[:, 2 * h + dk, :],
                                  start=(t == 0 and dk == 0), stop=(t == NS - 1 and dk == 1),
                                  tile_position=(0, 32 * h))
                last.then_inc(kc_used if t < NS - 1 else grp, 1)
            for h in range(HEADS):
                b = begin(("pT", h))
                for mt in range(2):
                    for t in range(2):
                        pe.wait_ge(emptied, G[("s", t, h // 2)] + 1)
                        last = turn(b[:, 256 * mt + P * t:256 * mt + P * t + P], probs[:, t, h, P * mt:P * mt + P], ident[:])
                last.then_inc(grp, 1)
            for m in range(KT):
                if m == 4:
                    b = begin("pST")
                    pe.wait_ge(emptied, G["sS"] + 1)
                    for mt in range(2):
                        last = turn(b[:, P * mt:P * mt + P], s_s[:, P * mt:P * mt + P], ident[:])
                    last.then_inc(grp, 1)
                b = begin(("o", m))
                pe.wait_ge(emptied, G[("pT", m // 2)] + 1)
                for mt in range(2):
                    last = mm(b[:, 0:NP_], v_mem[:, mt, P * m:P * m + P], probs_t[:, m // 2, mt, :],
                              start=(mt == 0), stop=(mt == 1))
                last.then_inc(grp, 1)
            b = begin("oS")
            pe.wait_ge(pd_ready, 8)
            for t in range(NS):
                values = chunk(("vc", t)).rearrange("p (m n) -> p m n", m=2)
                for mt in range(2):
                    for h in range(HEADS):
                        last = mm(b[32 * h:32 * h + 32, 0:256], p_diag[:, t, mt, h, :], values[:, mt, 256 * h:256 * h + 256],
                                  start=(t == 0 and mt == 0), stop=(t == NS - 1 and mt == 1),
                                  tile_position=(0, 32 * h))
                last.then_inc(vc_used if t < NS - 1 else grp, 1)
            b = begin("oST")
            pe.wait_ge(emptied, G["oS"] + 1)
            for dk in range(2):
                last = turn(b[:, P * dk:P * dk + P], o_s[:, P * dk:P * dk + P], ident[:])
            last.then_inc(grp, 1)
            pe.wait_ge(emptied, G["oST"] + 1)
            pe.wait_ge(os_ready, 1)
            for m in range(KT):
                project("w_xo", m, lambda k: o_fm[:, k, :], "xo")
            b = begin("lg")
            for k in range(KT):
                pe.wait_ge(h_ready, 2 * KT + k + 1)
                last = mm(b[0:NE, 0:T], router[:, k, :], h_fm[:, k, :], start=(k == 0), stop=(k == KT - 1))
            last.then_inc(grp, 1)
            sum_squares("ssq2", 4, 0, TT)
            b = begin("lgT")
            pe.wait_ge(emptied, G["lg"] + 1)
            for t in range(TT):
                last = turn(b[:, NE * t:NE * t + NE], lT[:, P * t:P * t + P], ident[0:NE, 0:NE])
            last.then_inc(grp, 1)
            for n in range(6):
                b = begin(("htok", n))
                width = P if n < 4 else NS
                for f in range(4):
                    last = turn(b[0:width, P * f:P * f + P],
                                h_fm[:, 4 * (n % 2) + f, P * (n // 2):P * (n // 2) + width], ident[:])
                last.then_inc(grp, 1)
            b = begin("rank")
            pe.wait_ge(sel_ready, 1)
            mm(b[:, 0:128], before[:], gt4[:].rearrange("p a e -> p (a e)"), start=True, stop=False)
            for s in range(TT):
                later = gt[:, s:s + 1, :].to_broadcast([P, TT - s, NE])
                last = mm(b[:, NE * (s + 1):128].rearrange("p (a e) -> p a e", e=NE), ones[:], later,
                          start=False, stop=(s == TT - 1))
            last.then_inc(grp, 1)
            b = begin("gT")
            pe.wait_ge(gate_ready, 1)
            for t in range(TT):
                last = turn(b[0:NE, P * t:P * t + P], gate[:, t, :], ident[:])
            last.then_inc(grp, 1)

            def gather(b, n):
                for half in range(2):
                    f = 2 * n + half
                    for t in range(TT):
                        last = mm(b[:, 256 * half:256 * half + 256], h_tok[:, t, P * f:P * f + P], p_hot[:, t, :],
                                  start=(t == 0), stop=(t == TT - 1))
                return last

            pe.wait_ge(p_built, 1)
            pe.wait_ge(late_zero, 5)
            pe.wait_ge(tok_copied, 6)
            for n in range(4):
                gather(begin(("ga", n)), n).then_inc(grp, 1)
            pe.wait_ge(bdn_in, 16)
            pe.wait_ge(emptied, NG)

            def combine(n, r, m, pair, biased=False):
                if r == 0:
                    pe.wait_ge(c_added, n + 1)
                elif r >= 2:
                    pe.wait_ge(c_added, n + r - 1 + 1)
                if biased:
                    mm(ps[:, 6 + m % 2, 0:T], bdn[:, P * m:P * m + P], gate_t[:], start=True, stop=False)
                mm(ps[:, 6 + m % 2, 0:T], y_hot[:, pair, P * m:P * m + P], g_hot[:, pair, :],
                   start=not biased, stop=True).then_inc(c_filled, 1)

            pe.wait_ge(iters_ready, 1)
            end = pe.value_load(iters[0:1, 0:1], min_val=4, max_val=20)
            with pe.Fori(0, end) as it:
                for j in range(8):
                    e, i, cur = it * 8 + j, j % 4, j // 4
                    quad = it * 2 + cur

                    def expert_chunk(c):
                        s = slot_of(c)
                        pe.wait_ge(landed[s], e * 16 + 16 * (front_uses(s) + 1))
                        return ring[:, s, :]

                    pe.wait_ge(gu_copied, e + 1)
                    if i == 0:
                        pe.wait_ge(side_copied, quad * 6 + 1)
                    for k in range(KT):
                        w = expert_chunk(k)
                        for n in range(2):
                            for h in range(2):
                                last = mm(ps[64 * h:64 * h + 64, n, :], xg[:, cur, k, SLOTS * i:SLOTS * i + SLOTS],
                                          w[:, D * h + 512 * n:D * h + 512 * n + 512], start=(k == 0), stop=(k == KT - 1))
                        last.then_inc(w_used if k < KT - 1 else gu_done, 1)
                    pos = quad * 6 + (0, 2, 3, 5)[i]
                    if i % 2 == 0:
                        pe.wait_ge(side_copied, pos + 1)
                        pe.wait_ge(w_built, quad + 1)
                        for t in range(TT):
                            width = P if t < 2 else NS
                            last = turn(ps[:, 5, P * t:P * t + width], w_hot[0:width, t, P * (i // 2):P * (i // 2) + P],
                                        ident[0:width, 0:width])
                        last.then_inc(side_filled, 1)
                        pos = pos + 1
                    pair = 1 - i // 2
                    if i == 0:
                        pe.wait_ge(y_copied, quad * 4 + 1)
                    if i == 2:
                        pe.wait_ge(y_copied, quad * 4 + 3)
                    biased = j in (4, 5)
                    if j == 4:
                        pe.wait_ge(gates_zero, it + 1)
                    for r in range(2):
                        combine(e * 4, r, 4 * (i % 2) + r, pair, biased)
                    pe.wait_ge(gu_copied, e + 2)
                    pe.wait_ge(t_read, e * 2 + 1)
                    for f in range(KT):
                        last = turn(ps[:, 2 + f // 4, P * (f % 4):P * (f % 4) + P], gu_sb[:, P * f:P * f + P], ident[:])
                    last.then_inc(t_done, 1)
                    pe.wait_ge(side_copied, pos + 1)
                    pe.wait_ge(p_built, quad + 2)
                    gather(ps[:, 5, :], i).then_inc(side_filled, 1)
                    for r in range(2, 4):
                        combine(e * 4, r, 4 * (i % 2) + r, pair, biased)
                    pe.wait_ge(hid_ready, e + 1)
                    pe.wait_ge(y_copied, e + 1)
                    for c in range(8, RING):
                        w = expert_chunk(c)
                        for kk in range(2):
                            k = 2 * (c - 8) + kk
                            for h in range(2):
                                last = mm(ps[64 * h:64 * h + 64, 4, :], hid[:, k, :],
                                          w[:, D * kk + 512 * h:D * kk + 512 * h + 512], start=(k == 0), stop=(k == KT - 1))
                        last.then_inc(w_used if c < RING - 1 else d_done, 1)
            pe.wait_ge(y_copied, end * 8 + 1)
            pe.wait_ge(c_added, end * 32 + 1)
            pe.wait_ge(side_copied, end * 12 + 1)
            for m in range(KT):
                mm(ps[:, (0, 1, 2, 3, 5, 6, 7, 4)[m], 0:T], y_hot[:, 1, P * m:P * m + P], g_hot[:, 1, :],
                   start=True, stop=True).then_inc(c_filled, 1)
            pe.wait_ge(sum_ready, 5)
            mm(ps[:, 0, 0:T], ones[:], ssum[:, 0:T], start=True, stop=True).then_inc(final_ssq, 1)


def feature_major(a):
    return np.ascontiguousarray(a.reshape(a.shape[0], -1, P).transpose(2, 1, 0))


def weight_chunks(w):
    k, n = w.shape[0] // P, w.shape[1] // 256
    return np.ascontiguousarray(w.reshape(k, P, n, 256).transpose(2, 1, 0, 3)).reshape(n, P, k * 256)


def kernel(**inputs):
    import concourse.bacc as bacc
    from concourse.bass_utils import run_bass_kernel_spmd

    a = {k: np.asarray(v) for k, v in inputs.items()}
    vec = lambda v: v.reshape(-1, P).T
    heads = lambda v: np.repeat(v, 64, axis=0)
    small = {
        "g_mix": vec(a["g_mix"]), "g_xattn": vec(a["g_xattn"]), "g_mem": vec(a["g_mem"]), "g_moe": vec(a["g_moe"]),
        "g_final": vec(a["g_final"]), "g_v": vec(a["g_v"]), "w_conv": vec(a["w_conv"]),
        "w00": vec(heads(a["w_spatial"][0, :, 0, 0])),
        "state": a["state_conv"][0].reshape(NS, 2, 4, P).transpose(3, 2, 1, 0).reshape(P, 64),
        "b_sp": heads(a["b_spatial"][0]).reshape(4, P, P).transpose(1, 0, 2).reshape(P, 512),
        "b_gu": a["b_gate_up"][0].reshape(NE, 16, P).transpose(2, 0, 1).reshape(P, 512),
        "b_router": np.broadcast_to(a["b_router"], (P, NE)),
        "router": a["w_router"][0].reshape(KT, P, NE).transpose(1, 0, 2).reshape(P, 256),
    }
    x = np.concatenate([a["x_prompt"][0], a["x_sample"][:, 0]], axis=0)
    kc = a["cache_mem_k"][0].reshape(NS, NMEM, KT, P).transpose(0, 3, 2, 1).reshape(NS, P, SLOT)
    vc = a["cache_mem_v"][0].reshape(NS, 2, P, D).transpose(0, 2, 1, 3).reshape(NS, P, SLOT)
    arrays = {
        "x_t": feature_major(x), "mem_t": feature_major(a["mem_prompt"][0]),
        "w_k": weight_chunks(a["w_k"][0]), "w_v": weight_chunks(a["w_v"][0]), "w_in": weight_chunks(a["w_in"][0]),
        "w_out": weight_chunks(a["w_out"][0]), "w_q": weight_chunks(a["w_q"][0]), "w_xo": weight_chunks(a["w_xo"][0]),
        "kc": np.ascontiguousarray(kc), "vc": np.ascontiguousarray(vc),
        "w_gu": a["w_gate_up"][0].reshape(NE, KT, P, 2 * D), "w_dn": a["w_down"][0].reshape(NE, KT, P, D),
        "params": np.ascontiguousarray(np.concatenate([small[n] for n, _ in PARAM_WIDTH], axis=1)),
        "ws_t": np.ascontiguousarray(a["w_spatial"][0].transpose(2, 0, 1)),
        "b_down": a["b_down"][0],
    }
    outs = {"y_t": (P, KT, T), "mk_t": (P, KT, NMEM), "mv": (P, 2, D), "conv_p": (P, 4, 2),
            "conv_s": (P, 4, 2, NS), "chunk_v": (P, 4, NS)}
    nc = bacc.Bacc("TRN2", target_bir_lowering=False, num_devices=1)
    args, given = [], {}
    for name, v in arrays.items():
        given[f"in_{name}"] = np.ascontiguousarray(v)
        args.append(nc.dram_tensor(f"in_{name}", v.shape, F32, kind="ExternalInput").ap())
    for name, shape in outs.items():
        args.append(nc.dram_tensor(f"out_{name}", shape, F32, kind="ExternalOutput").ap())
    build(nc, *args)
    got = run_bass_kernel_spmd(nc, [given], core_ids=[0]).results[0]
    y = got["out_y_t"].transpose(2, 1, 0).reshape(T, D)
    mk = got["out_mk_t"].transpose(2, 1, 0).reshape(1, 1, NMEM, HEADS, NMEM)
    v_m = got["out_mv"].transpose(1, 0, 2).reshape(1, 1, NMEM, HEADS, NMEM)
    conv_p = got["out_conv_p"].transpose(2, 1, 0).reshape(1, 1, 2, 512)
    conv_s = got["out_conv_s"].transpose(3, 2, 1, 0).reshape(1, NS, 2, 512)
    chunk_v = got["out_chunk_v"].transpose(2, 1, 0).reshape(1, NS, 1, 8, 64)
    return (np.ascontiguousarray(y[:NP_]).reshape(1, NP_, D), np.ascontiguousarray(y[NP_:]).reshape(NS, 1, D),
            np.ascontiguousarray(mk), np.ascontiguousarray(v_m), np.ascontiguousarray(conv_p),
            np.ascontiguousarray(conv_s), np.ascontiguousarray(chunk_v))
```
